# Optimizing a Trainium2 kernel written in Bass

```python
import jax, jax.numpy as jnp
from jax import lax
import numpy as np

D_MODEL = 2048
BATCH = 1
SEQ = 256
DEPTH = 1

N_HEADS = 16
Q_LORA_RANK = 512
KV_LORA_RANK = 512
QK_NOPE_DIM = 128
QK_ROPE_DIM = 64
V_HEAD_DIM = 128
ROPE_THETA = 10000.0
ATTN_WIDTH = N_HEADS * V_HEAD_DIM
Q_BLOCK = 128
POOL_WIDTH = D_MODEL // 2
POOL_WINDOWS = (2, 4, 8, 16)
POOL_GROUPS = len(POOL_WINDOWS)
POOL_GROUP_DIM = POOL_WIDTH // POOL_GROUPS
N_MEM = 256
MEM_HEADS = 4
MEM_HEAD_DIM = D_MODEL // MEM_HEADS
D_FF = 5632
CONV_WIDTH = 3
EPS = 1e-6
IN_SIZES = (Q_LORA_RANK, KV_LORA_RANK, QK_ROPE_DIM, POOL_WIDTH, D_MODEL, D_MODEL)
D_IN = Q_LORA_RANK + KV_LORA_RANK + QK_ROPE_DIM + POOL_WIDTH + 2 * D_MODEL

kernel_name = "hybrid_mla_pool_memxattn_convffn"

def rmsnorm(x, g):
    xf = x.astype(jnp.float32)
    y = xf * lax.rsqrt(jnp.mean(xf * xf, axis=-1, keepdims=True) + EPS)
    return (y * g.astype(jnp.float32)).astype(x.dtype)

def rope_tables(positions, dtype):
    inv_freq = ROPE_THETA ** (-jnp.arange(0, QK_ROPE_DIM, 2, dtype=jnp.float32) / QK_ROPE_DIM)
    ang = positions.astype(jnp.float32)[..., None] * inv_freq
    return jnp.cos(ang).astype(dtype), jnp.sin(ang).astype(dtype)

def apply_rope(x, cos, sin):
    half = QK_ROPE_DIM // 2
    x1, x2 = x[..., :half], x[..., half:]
    return jnp.concatenate([x1 * cos - x2 * sin, x2 * cos + x1 * sin], axis=-1)

def split_cols(z, sizes):
    outs, start = [], 0
    for n in sizes:
        outs.append(z[..., start:start + n])
        start += n
    return outs

def mla_branch(q_lat, c_kv, k_pe, positions, g_q_a, w_q_b, g_kv_a, w_kv_b):
    B, S, _ = q_lat.shape
    q = (rmsnorm(q_lat, g_q_a) @ w_q_b).reshape(B, S, N_HEADS, QK_NOPE_DIM + QK_ROPE_DIM)
    q_nope, q_pe = q[..., :QK_NOPE_DIM], q[..., QK_NOPE_DIM:]
    kv = (rmsnorm(c_kv, g_kv_a) @ w_kv_b).reshape(B, S, N_HEADS, QK_NOPE_DIM + V_HEAD_DIM)
    k_nope, v = kv[..., :QK_NOPE_DIM], kv[..., QK_NOPE_DIM:]
    cos, sin = rope_tables(positions, q.dtype)
    q_pe = apply_rope(q_pe, cos[:, :, None, :], sin[:, :, None, :])
    k_pe = apply_rope(k_pe, cos, sin)
    scale = (QK_NOPE_DIM + QK_ROPE_DIM) ** -0.5
    nb = S // Q_BLOCK
    qn_b = q_nope.reshape(B, nb, Q_BLOCK, N_HEADS, QK_NOPE_DIM).transpose(1, 0, 3, 2, 4)
    qp_b = q_pe.reshape(B, nb, Q_BLOCK, N_HEADS, QK_ROPE_DIM).transpose(1, 0, 3, 2, 4)
    kn = k_nope.transpose(0, 2, 1, 3)
    vh = v.transpose(0, 2, 1, 3)
    key_idx = jnp.arange(S)

    def query_block(args):
        qn, qp, i = args
        s = (jnp.einsum('bhqd,bhkd->bhqk', qn, kn)
             + jnp.einsum('bhqr,bkr->bhqk', qp, k_pe)).astype(jnp.float32) * scale
        q_idx = i * Q_BLOCK + jnp.arange(Q_BLOCK)
        s = jnp.where(key_idx[None, :] <= q_idx[:, None], s, -jnp.inf)
        p = jax.nn.softmax(s, axis=-1).astype(vh.dtype)
        return jnp.einsum('bhqk,bhkd->bhqd', p, vh)

    o = lax.map(query_block, (qn_b, qp_b, jnp.arange(nb)))
    return o.transpose(1, 0, 3, 2, 4).reshape(B, S, ATTN_WIDTH)

def pool_branch(u, w_pool_grp, pool_scale):
    B, S, _ = u.shape
    ug = u.reshape(B, S, POOL_GROUPS, POOL_GROUP_DIM).astype(jnp.float32)
    cs = jnp.concatenate([jnp.zeros((B, 1, POOL_GROUPS, POOL_GROUP_DIM), jnp.float32),
                          jnp.cumsum(ug, axis=1)], axis=1)
    t = jnp.arange(S)
    outs = []
    for g, w in enumerate(POOL_WINDOWS):
        lo = jnp.maximum(t + 1 - w, 0)
        win_sum = cs[:, 1:, g] - cs[:, lo, g]
        cnt = jnp.minimum(t + 1, w).astype(jnp.float32)[None, :, None]
        outs.append(win_sum / cnt - ug[:, :, g])
    d = jnp.stack(outs, axis=2).astype(u.dtype)
    y = jnp.einsum('bsgc,gcd->bsgd', d, w_pool_grp).reshape(B, S, POOL_WIDTH)
    return y * pool_scale

def memory_xattn(h, mem_n, w_mem_q, w_mem_kv, w_mem_o):
    B, S, _ = h.shape
    q = (h @ w_mem_q).reshape(B, S, MEM_HEADS, MEM_HEAD_DIM)
    kv = (mem_n @ w_mem_kv).reshape(B, N_MEM, 2, MEM_HEADS, MEM_HEAD_DIM)
    k, v = kv[:, :, 0], kv[:, :, 1]
    s = jnp.einsum('bqhd,bkhd->bhqk', q, k).astype(jnp.float32) * (MEM_HEAD_DIM ** -0.5)
    p = jax.nn.softmax(s, axis=-1).astype(v.dtype)
    o = jnp.einsum('bhqk,bkhd->bqhd', p, v).reshape(B, S, D_MODEL)
    return o @ w_mem_o

def conv_gated_ffn(h, w_ffn_in, conv_w, conv_b, w_ffn_out):
    S = h.shape[1]
    a = h @ w_ffn_in
    ap = jnp.pad(a, ((0, 0), (CONV_WIDTH - 1, 0), (0, 0)))
    c = conv_b
    for k in range(CONV_WIDTH):
        c = c + ap[:, k:k + S] * conv_w[k]
    gate, up = c[..., :D_FF], c[..., D_FF:]
    return (jax.nn.gelu(gate, approximate=True) * up) @ w_ffn_out

def setup_inputs(seed: int = 0) -> dict:
    key = jax.random.key(seed)
    ks = iter(jax.random.split(key, 40))
    L = DEPTH

    def w(shape, fan_in):
        return jax.random.normal(next(ks), shape, jnp.float32) * fan_in ** -0.5

    def gain(shape):
        return 1.0 + 0.05 * jax.random.normal(next(ks), shape, jnp.float32)

    x = jax.random.normal(next(ks), (BATCH, SEQ, D_MODEL), jnp.float32)
    mem = jax.random.normal(next(ks), (BATCH, N_MEM, D_MODEL), jnp.float32)
    offset = jax.random.randint(next(ks), (BATCH, 1), 0, 4096, jnp.int32)
    positions = (offset + jnp.arange(SEQ, dtype=jnp.int32)[None, :]).astype(jnp.int32)
    return {
        "x": x,
        "mem": mem,
        "positions": positions,
        "g_mix_pre": gain((L, D_MODEL)),
        "w_in": w((L, D_MODEL, D_IN), D_MODEL),
        "g_q_a": gain((L, Q_LORA_RANK)),
        "w_q_b": w((L, Q_LORA_RANK, N_HEADS * (QK_NOPE_DIM + QK_ROPE_DIM)), Q_LORA_RANK),
        "g_kv_a": gain((L, KV_LORA_RANK)),
        "w_kv_b": w((L, KV_LORA_RANK, N_HEADS * (QK_NOPE_DIM + V_HEAD_DIM)), KV_LORA_RANK),
        "w_attn_br": w((L, ATTN_WIDTH, D_MODEL), ATTN_WIDTH),
        "w_pool_grp": w((L, POOL_GROUPS, POOL_GROUP_DIM, POOL_GROUP_DIM), POOL_GROUP_DIM),
        "pool_scale": gain((L, POOL_WIDTH)),
        "w_pool_br": w((L, POOL_WIDTH, D_MODEL), POOL_WIDTH),
        "w_mix_out": w((L, D_MODEL, D_MODEL), D_MODEL),
        "g_mix_post": gain((L, D_MODEL)),
        "g_mem_pre": gain((L, D_MODEL)),
        "g_mem_kv": gain((L, D_MODEL)),
        "w_mem_q": w((L, D_MODEL, D_MODEL), D_MODEL),
        "w_mem_kv": w((L, D_MODEL, 2 * D_MODEL), D_MODEL),
        "w_mem_o": w((L, D_MODEL, D_MODEL), D_MODEL),
        "g_mem_post": gain((L, D_MODEL)),
        "g_ffn_pre": gain((L, D_MODEL)),
        "w_ffn_in": w((L, D_MODEL, 2 * D_FF), D_MODEL),
        "conv_w": w((L, CONV_WIDTH, 2 * D_FF), CONV_WIDTH),
        "conv_b": 0.01 * jax.random.normal(next(ks), (L, 2 * D_FF), jnp.float32),
        "w_ffn_out": w((L, D_FF, D_MODEL), D_FF),
        "g_ffn_post": gain((L, D_MODEL)),
    }

def reference(x, mem, positions, g_mix_pre, w_in, g_q_a, w_q_b, g_kv_a, w_kv_b,
              w_attn_br, w_pool_grp, pool_scale, w_pool_br, w_mix_out, g_mix_post,
              g_mem_pre, g_mem_kv, w_mem_q, w_mem_kv, w_mem_o, g_mem_post,
              g_ffn_pre, w_ffn_in, conv_w, conv_b, w_ffn_out, g_ffn_post):
    for l in range(DEPTH):
        h = rmsnorm(x, g_mix_pre[l])
        z = h @ w_in[l]
        q_lat, c_kv, k_pe, u_pool, gate_a, gate_p = split_cols(z, IN_SIZES)
        y_a = mla_branch(q_lat, c_kv, k_pe, positions, g_q_a[l], w_q_b[l],
                         g_kv_a[l], w_kv_b[l]) @ w_attn_br[l]
        y_p = pool_branch(u_pool, w_pool_grp[l], pool_scale[l]) @ w_pool_br[l]
        merged = jax.nn.sigmoid(gate_a) * y_a + jax.nn.sigmoid(gate_p) * y_p
        x = x + rmsnorm(merged @ w_mix_out[l], g_mix_post[l])
        h = rmsnorm(x, g_mem_pre[l])
        mem_n = rmsnorm(mem, g_mem_kv[l])
        x = x + rmsnorm(memory_xattn(h, mem_n, w_mem_q[l], w_mem_kv[l], w_mem_o[l]),
                        g_mem_post[l])
        h = rmsnorm(x, g_ffn_pre[l])
        x = x + rmsnorm(conv_gated_ffn(h, w_ffn_in[l], conv_w[l], conv_b[l], w_ffn_out[l]),
                        g_ffn_post[l])
    return x


_drawn_inputs = setup_inputs


def setup_inputs(seed=0):
    import zlib

    import numpy as np

    out = dict(_drawn_inputs(seed))
    spreads = {}
    factors = {'g_q_a': 7.245, 'g_kv_a': 4.976, 'conv_b': 7.934, 'pool_scale': 7.794}
    for name, (base, spread) in spreads.items():
        noise = np.random.default_rng([zlib.crc32(name.encode()), seed]).standard_normal(out[name].shape)
        drawn = base * np.exp(spread * noise) if base else spread * noise
        out[name] = __import__('jax').numpy.asarray(drawn.astype(out[name].dtype))
    for name, factor in factors.items():
        out[name] = (out[name] * factor).astype(out[name].dtype)
    return out
```

```python
from contextlib import ExitStack

import numpy as np

import concourse.bass as bass
from concourse import mybir

ALU = mybir.AluOpType
ACT = mybir.ActivationFunctionType
AX = mybir.AxisListType
F32 = mybir.dt.float32
F32R = mybir.dt.float32r
I32 = mybir.dt.int32

P = 128
NEG = -1.0e30
THETA = 10000.0
EPS = 1e-6
WINDOWS = (2, 4, 8, 16)
RAW_SLOTS = 4
AHEAD = 4
TWO_PI_A = 6.28125
TWO_PI_B = 0.0019350051879882812
TWO_PI_C = float(2 * np.pi - TWO_PI_A - TWO_PI_B)
ROUND = 12582912.0


def hybrid_layer(nc, a, out, x3_spill):
    S, D = a["x"].shape[1:]
    TT = S // P
    KD = D // P
    QL = a["w_q_b"].shape[1]
    KL = QL // P
    NH = 16
    NOPE, ROPE, VD = 128, 64, 128
    HALF = ROPE // 2
    PW = a["w_pool_br"].shape[1]
    KP = PW // P
    DFF = a["w_ffn_out"].shape[1]
    KF = DFF // P
    NC = 512
    ND = D // NC
    NF = DFF // NC
    QPAIR = 2 * (NOPE + ROPE)
    SCALE = float((NOPE + ROPE) ** -0.5)
    MHD = D // 4
    MSCALE = float(MHD ** -0.5)

    V_LAT = 0
    V_POOLIN = V_LAT + 2 * KD // 2
    V_KPE = V_POOLIN + 2 * KD // 2
    V_GRP = V_KPE + 4
    V_YP = V_GRP + 4
    V_ATT = V_YP + ND * KP // 2
    V_YA = V_ATT + NH // 2 * 12
    V_MIX = V_YA + ND * 8
    V_MKV = V_MIX + ND * 8
    V_MQ = V_MKV + 2 * ND * 8
    V_MO = V_MQ + ND * 8
    V_FIN = V_MO + ND * 8
    V_FOUT = V_FIN + 2 * NF * 8
    N_UNITS = V_FOUT + ND * 24

    U_LAT, U_POOLIN, U_KPE, U_YP, U_ATT = 0, 2, 4, 5, 9
    U_YA = U_ATT + 3 * NH // 2
    U_MIX = U_YA + ND
    U_MKV = U_MIX + ND
    U_MQ = U_MKV + 2 * ND
    U_MO = U_MQ + ND
    U_FIN = U_MO + ND
    U_FOUT = U_FIN + 2 * NF

    T_X, T_Q, T_C, T_D, T_Y, T_O = 0, 8, 10, 12, 16, 20
    T_MRG = T_O + NH // 2
    T_MEM = T_MRG + 8
    T_X2 = T_MEM + 8
    T_MOUT = T_X2 + 8
    T_X3 = T_MOUT + 8

    A_SET, A_KPE, A_PAIR = 0, 2, 3
    A_MK = A_PAIR + 5 * NH // 2
    A_MQ = A_MK + 2 * ND

    N_X, N_Q, N_C, N_MEM, N_Y1, N_X2, N_Y2, N_X3, N_Y3 = range(9)

    G_MIX, G_MEM, G_MEMKV, G_FFN = 0, KD, 2 * KD, 3 * KD
    G_Q, G_KV, G_POOL = 4 * KD, 4 * KD + KL, 4 * KD + 2 * KL
    NG = 4 * KD + 2 * KL + KP

    def rows(name):
        return a[name][0].rearrange("(k p) n -> p k n", p=P)

    w_in, w_qb, w_kvb = rows("w_in"), rows("w_q_b"), rows("w_kv_b")
    w_grp = a["w_pool_grp"][0].rearrange("g (c p) d -> p (g c) d", p=P)
    C_Q, C_C, C_PE, C_U = 0, QL, 2 * QL, 2 * QL + ROPE
    C_GA, C_GP = C_U + PW, C_U + PW + D
    tok = a["x"][0].rearrange("(t p) d -> p t d", p=P)
    memtok = a["mem"][0].rearrange("(t p) d -> p t d", p=P)
    outtok = out[0].rearrange("(t p) d -> p t d", p=P)

    ctx = ExitStack()

    def sb(scope, name, shape, dt=F32):
        return scope.enter_context(nc.sbuf_tensor(name, shape, dt))

    def sem(name):
        return ctx.enter_context(nc.semaphore(name))

    raw = sb(ctx, "raw", [P, RAW_SLOTS, 2, 2 * NC])
    whi = sb(ctx, "whi", [P, AHEAD, 2 * NC], F32R)
    wlo = sb(ctx, "wlo", [P, AHEAD, 2 * NC], F32R)
    ident = sb(ctx, "ident", [P, P])
    gcol = sb(ctx, "gcol", [P, NG])
    ccol = sb(ctx, "ccol", [P, 4, 2 * KF])
    part = sb(ctx, "part", [P, 9, TT, 4])
    ssq = sb(ctx, "ssq", [P, 9, TT])
    var = sb(ctx, "var", [P, 9, TT])
    std = sb(ctx, "std", [P, 9, TT])
    rstd = sb(ctx, "rstd", [P, 9, TT])
    life_a = ExitStack()
    actA = sb(life_a, "actA", [P, 2, KD, S], F32R)
    mixmem = ExitStack()
    actB = sb(mixmem, "actB", [P, 2, KD, S], F32R)
    bufX = sb(mixmem, "bufX", [P, TT, D])
    bufY = sb(mixmem, "bufY", [P, TT, D])
    mix = ExitStack()
    lat = sb(mix, "lat", [P, 2, 2 * KL, S], F32R)
    mask = sb(mix, "mask", [P, 3 * P])
    cosT = sb(mix, "cosT", [P, TT, HALF])
    sinT = sb(mix, "sinT", [P, TT, HALF])
    kpeT = sb(mix, "kpeT", [ROPE, S])
    ropet = sb(mix, "ropet", [P, 4, TT * 2 * HALF])
    early = ExitStack()
    grow = sb(early, "grow", [NG, P])
    crow = sb(early, "crow", [2 * KF, 4, P])
    zlat = sb(early, "zlat", [P, 2, TT, QL])
    kpe = sb(early, "kpe", [P, TT, ROPE])
    pm0 = sb(early, "pm0", [P, 4, S])
    pm1 = sb(early, "pm1", [P, 4, P])
    pos_i = sb(early, "pos_i", [P, TT], I32)
    posf = sb(early, "posf", [P, TT])
    invf = sb(early, "invf", [P, HALF])
    ang = sb(early, "ang", [P, TT, HALF])
    turns = sb(early, "turns", [P, TT, HALF])
    early.close()
    pairs = ExitStack()
    q_sb = sb(pairs, "q_sb", [P, TT, QPAIR])
    kv_sb = sb(pairs, "kv_sb", [P, TT, NC])
    qkT = sb(pairs, "qkT", [P, 2, 2 * S])
    qpeT = sb(pairs, "qpeT", [ROPE, 2, S])
    prob = sb(pairs, "prob", [P, 2, 3 * P])
    probT = sb(pairs, "probT", [P, 2, 3 * P])
    gp_sb = sb(pairs, "gp_sb", [P, TT, NC])
    smax = sb(pairs, "smax", [P, 2, TT])
    nmax = sb(pairs, "nmax", [P, 2, TT])
    ssum = sb(pairs, "ssum", [P, 2, TT])
    rsum = sb(pairs, "rsum", [P, 2, TT])
    pairs.close()
    mix.close()
    memp = ExitStack()
    memk = sb(memp, "memk", [P, KD, S])
    memv = sb(memp, "memv", [P, TT, D])
    kch = sb(memp, "kch", [P, TT, NC])
    mmax = sb(memp, "mmax", [P, TT])
    mnmax = sb(memp, "mnmax", [P, TT])
    msum = sb(memp, "msum", [P, TT])
    mrsum = sb(memp, "mrsum", [P, TT])
    memp.close()
    mixmem.close()
    ffn = ExitStack()
    gT = sb(ffn, "gT", [P, 2, KF, S], F32R)
    a_sb = sb(ffn, "a_sb", [P, 2, TT, NC])
    cg = sb(ffn, "cg", [P, 4, S])
    cu = sb(ffn, "cu", [P, 4, S])
    ffn.close()
    life_a.close()
    tail = ExitStack()
    y3 = sb(tail, "y3", [P, TT, D])
    x3 = sb(tail, "x3", [P, TT, D])
    tail.close()
    gpost = memv[:, 0, :]
    gpost3 = a_sb[:, :, :, :].rearrange("p a t n -> p (a t n)")
    mq_sb = bufY[:, :, 0:NC]
    mv_sb = bufY[:, :, NC:2 * NC]
    mp_sb = bufY[:, :, 2 * NC:2 * NC + S]
    mpT = bufY[:, :, 3 * NC:3 * NC + S]
    mqT = kch[:, :, :].rearrange("p t n -> p (t n)").rearrange("p (d s) -> p d s", s=S)

    bank = [ctx.enter_context(nc.psum_tensor(f"bank{i}", [P, 512], F32)) for i in range(8)]
    acc = bank[0:2]
    tr = bank[2:4]
    sc = bank[4:6]
    at = bank[6:8]

    w_loaded = [sem(f"w_loaded{s}") for s in range(RAW_SLOTS)]
    hi_done, lo_done, w_used = sem("hi_done"), sem("lo_done"), sem("w_used")
    acc0_ready = sem("acc0_ready")
    acc_out = [sem("acc0_out"), sem("acc1_out")]
    t_filled, t_hi, t_out = sem("t_filled"), sem("t_hi"), sem("t_out")
    at_filled, at_out = sem("at_filled"), sem("at_out")
    x_in = [sem("x_in0"), sem("x_in1")]
    g_in, c_in, pos_in = sem("g_in"), sem("c_in"), sem("pos_in")
    ident_ok, consts_ok, pm_ok, pm_step = sem("ident_ok"), sem("consts_ok"), sem("pm_ok"), sem("pm_step")
    part_zero, cols_ok = sem("part_zero"), sem("cols_ok")
    sq_done, sum_done, var_done, std_done, rstd_done = (sem(n) for n in (
        "sq_done", "sum_done", "var_done", "std_done", "rstd_done"))
    rope_step, trig_ok, abs_ok, rope_ok, ang_ok = (sem(n) for n in (
        "rope_step", "trig_ok", "abs_ok", "rope_ok", "ang_ok"))
    s_filled, s_max, s_nmax, s_exp, s_rsum, s_norm = (sem(n) for n in (
        "s_filled", "s_max", "s_nmax", "s_exp", "s_rsum", "s_norm"))
    mp_ok = sem("mp_ok")
    mrg_mul, mrg_ok = sem("mrg_mul"), sem("mrg_ok")
    mem_in, x_again, gpost_in = sem("mem_in"), sem("x_again"), sem("gpost_in")
    y_gained, res_done = sem("y_gained"), sem("res_done")
    mv_ok, m_filled, m_max, m_nmax, m_exp, m_rsum, m_norm = (sem(n) for n in (
        "mv_ok", "m_filled", "m_max", "m_nmax", "m_exp", "m_rsum", "m_norm"))
    mpT_filled, mpT_out = sem("mpT_filled"), sem("mpT_out")
    spill, x3_in, stored = sem("spill"), sem("x3_in"), sem("stored")
    ga_filled, ua_filled, conv_step, gconv, uconv, gelu_ok, f_mul, f_hi, f_lo = (sem(n) for n in (
        "ga_filled", "ua_filled", "conv_step", "gconv", "uconv", "gelu_ok", "f_mul", "f_hi", "f_lo"))

    def filled(f):
        return f + 1 if isinstance(f, int) and f < T_Y else f + 1 - 4

    def width(v):
        if V_KPE <= v < V_GRP:
            return 4 * ROPE
        if V_GRP <= v < V_YP:
            return 4 * P
        if v >= V_FOUT and (v - V_FOUT) % 6 == 5:
            return NC
        return 2 * NC

    def f32(ap):
        return ap.bitcast(F32)

    SQ = {}
    count = 0
    for n, parts in ((N_X, 8), (N_Q, 2), (N_C, 2), (N_MEM, 8), (N_Y1, 8), (N_X2, 8), (N_Y2, 8), (N_X3, 8), (N_Y3, 8)):
        SQ[n] = count
        count += parts

    block = ctx.enter_context(nc.Block())

    @block.sync
    def _(sp):
        def load(c, cs, src, n, kts=4):
            s = cs % RAW_SLOTS
            if not (isinstance(c, int) and c < RAW_SLOTS):
                sp.wait_ge(lo_done, 2 * c - 2 * RAW_SLOTS + 2)
            if n == NC:
                dst = raw[:, s, :, :].rearrange("p u (k n) -> p (u k) n", n=n)[:, 0:kts, :]
                sp.dma_start(dst, src).then_inc(w_loaded[s], 32)
            else:
                per = kts // 2
                for h in range(2):
                    dst = raw[:, s, h, 0:per * n].rearrange("p (k n) -> p k n", n=n)
                    sp.dma_start(dst, src[:, h * per:(h + 1) * per, :]).then_inc(w_loaded[s], 16)

        for name, row, k in (("g_mix_pre", G_MIX, KD), ("g_mem_pre", G_MEM, KD), ("g_mem_kv", G_MEMKV, KD),
                             ("g_ffn_pre", G_FFN, KD), ("g_q_a", G_Q, KL), ("g_kv_a", G_KV, KL),
                             ("pool_scale", G_POOL, KP)):
            sp.dma_start(grow[row:row + k, :], a[name][0].rearrange("(k p) -> k p", p=P)).then_inc(g_in, 16)
        for h in range(2):
            sp.dma_start(bufX[:, :, h * D // 2:(h + 1) * D // 2],
                         tok[:, :, h * D // 2:(h + 1) * D // 2]).then_inc(x_in[h], 16)

        def column(c, w, col, n=NC, kd=KD):
            for j in range(kd // 4):
                load(c + j, j, w[:, 4 * j:4 * j + 4, bass.ds(col, n)], n)

        for n in range(2):
            column(V_LAT // 2 + 4 * n, w_in, C_Q + n * NC)
        for n in range(2):
            column(V_POOLIN // 2 + 4 * n, w_in, C_U + n * NC)
        for j in range(2):
            load(V_KPE // 2 + j, j, w_in[:, 8 * j:8 * j + 8, C_PE:C_PE + ROPE], ROPE, 8)
        for j in range(2):
            load(V_GRP // 2 + j, 2 + j, w_grp[:, 4 * j:4 * j + 4, :], 2 * P)
        with sp.Fori(0, ND // 2) as i:
            for m in range(2):
                for j in range(2):
                    load(V_YP // 2 + 4 * i + 2 * m + j, 2 * m + j,
                         rows("w_pool_br")[:, 4 * j:4 * j + 4, bass.ds(i * 2 * NC + m * NC, NC)], NC)
        with sp.Fori(0, NH // 4) as i:
            for m in range(2):
                c = V_ATT // 2 + 12 * i + 6 * m
                load(c, 6 * m, w_qb[:, :, bass.ds(i * 2 * QPAIR + m * QPAIR, QPAIR)], QPAIR)
                load(c + 1, 6 * m + 1, w_kvb[:, :, bass.ds(i * 2 * NC + m * NC, NC)], NC)
                for j in range(4):
                    load(c + 2 + j, 6 * m + 2 + j,
                         w_in[:, 4 * j:4 * j + 4, bass.ds(i * NC + (C_GA, C_GP)[m], NC)], NC)
        for name, v, n in (("w_attn_br", V_YA, ND), ("w_mix_out", V_MIX, ND), ("w_mem_kv", V_MKV, 2 * ND),
                           ("w_mem_q", V_MQ, ND), ("w_mem_o", V_MO, ND)):
            with sp.Fori(0, n) as i:
                column(v // 2 + 4 * i, rows(name), i * NC)
        with sp.Fori(0, NF) as i:
            for m in range(2):
                column(V_FIN // 2 + 8 * i + 4 * m, rows("w_ffn_in"), i * NC + m * DFF)
        with sp.Fori(0, ND) as i:
            k = 0
            for j in range(12):
                kts = (4, 4, 3)[j % 3]
                load(V_FOUT // 2 + 12 * i + j, j, rows("w_ffn_out")[:, k:k + kts, bass.ds(i * NC, NC)], NC, kts)
                k += kts
        for q in range(8):
            t, o = q % 2, slice(q // 2 * NC, (q // 2 + 1) * NC)
            sp.wait_ge(res_done, 16 + q + 1)
            sp.dma_start(outtok[:, t, o], y3[:, t, o]).then_inc(stored, 16)
        sp.wait_ge(stored, 16 * 8)

    @block.gpsimd
    def _(pool):
        pool.memset(ident[:, :], 0.0).then_inc(pm_step, 1)
        pool.wait_ge(pm_step, 1)
        pool.affine_select(out=ident[:, :], in_=ident[:, :], compare_op=ALU.not_equal, fill=1.0, base=0,
                           pattern=[[-1, P]], channel_multiplier=1).then_inc(ident_ok, 1)
        freq = np.float32(THETA) ** (-np.arange(0, ROPE, 2, dtype=np.float32) / np.float32(ROPE))
        for j in range(HALF):
            last = pool.memset(invf[:, j:j + 1], float(freq[j]))
        last.then_inc(consts_ok, 1)
        for g, w in enumerate(WINDOWS):
            pool.memset(pm1[:, g, :], 1.0 / w)
            last = pool.memset(pm0[:, g, w - 1:S], 1.0 / w)
            for t in range(w - 1):
                last = pool.memset(pm0[:, g, t:t + 1], 1.0 / (t + 1))
        last.then_inc(pm_step, 1)
        pool.wait_ge(pm_step, 2)
        n = 2
        for g, w in enumerate(WINDOWS):
            for pm, width in ((pm0, S), (pm1, P)):
                pool.affine_select(out=pm[:, g, :], in_=pm[:, g, :], compare_op=ALU.is_ge, fill=0.0, base=0,
                                   pattern=[[1, width]], channel_multiplier=-1).then_inc(pm_step, 1)
                n += 1
                pool.wait_ge(pm_step, n)
                pool.affine_select(out=pm[:, g, :], in_=pm[:, g, :], compare_op=ALU.is_ge, fill=0.0, base=w - 1,
                                   pattern=[[-1, width]], channel_multiplier=1).then_inc(pm_step, 1)
                n += 1
                pool.wait_ge(pm_step, n)
                pool.tensor_tensor(pm[:, g, 0:P], pm[:, g, 0:P], ident[:, :], ALU.subtract).then_inc(pm_ok, 1)
        pool.memset(mask[:, :], 0.0).then_inc(mp_ok, 1)
        pool.wait_ge(mp_ok, 1)
        for b in (0, 2):
            last = pool.affine_select(out=mask[:, b * P:(b + 1) * P], in_=mask[:, b * P:(b + 1) * P],
                                      compare_op=ALU.is_ge, fill=NEG, base=0, pattern=[[-1, P]],
                                      channel_multiplier=1)
            last.then_inc(consts_ok, 1)
        with pool.Fori(0, ND) as i:
            for t in range(TT):
                pool.wait_ge(acc_out[t], U_ATT + 6 * i + 6)
                ya = bufY[:, t, bass.ds(i * NC, NC)]
                pool.tensor_tensor(ya, ya, gp_sb[:, t, :], ALU.mult).then_inc(mp_ok, 1)

        def post(n, y, gain, k):
            pool.wait_ge(gpost_in, 16 * (k + 1))
            for j in range(ND):
                for t in range(TT):
                    pool.wait_ge(sq_done, SQ[n] + 2 * j + t + 1)
                    ya = y[:, t, j * NC:(j + 1) * NC]
                    pool.tensor_tensor(ya, ya, gain[:, j * NC:(j + 1) * NC], ALU.mult).then_inc(y_gained, 1)

        post(N_Y1, bufY, gpost, 0)
        with pool.Fori(0, ND) as i:
            pool.wait_ge(acc_out[0], U_MQ + 1 + i)
            pool.wait_ge(acc_out[1], U_MQ + 1 + i)
            pool.tensor_copy(mv_sb, memv[:, :, bass.ds(i * NC, NC)]).then_inc(mv_ok, 1)
        post(N_Y2, bufY, gpost, 1)
        post(N_Y3, y3, gpost3, 2)

    @block.tensor
    def _(pe):
        def unit(v, vs, lhs, kts, n, u, first, last):
            s = vs % AHEAD
            pe.wait_ge(lo_done, v + 1)
            for t in range(TT):
                if first and not (isinstance(u, int) and u == 0):
                    pe.wait_ge(acc_out[t], u)
                for kk, k in enumerate(kts):
                    hi, lo = lhs(0, k)[:, t * P:(t + 1) * P], lhs(1, k)[:, t * P:(t + 1) * P]
                    wh, wl = whi[:, s, kk * n:(kk + 1) * n], wlo[:, s, kk * n:(kk + 1) * n]
                    f, l = first and kk == 0, last and kk == len(kts) - 1
                    pe.matmul(acc[t][:, 0:n], hi, wh, start=f, stop=False)
                    pe.matmul(acc[t][:, 0:n], hi, wl, start=False, stop=False)
                    mm = pe.matmul(acc[t][:, 0:n], lo, wh, start=False, stop=l)
                if last and t == 0:
                    mm.then_inc(acc0_ready, 1)
            mm.then_inc(w_used, 1)

        def lhsA(part_, k):
            return actA[:, part_, k, :]

        def lhsB(part_, k):
            return actB[:, part_, k, :]

        def t_wait(f):
            if not (isinstance(f, int) and f < 2):
                pe.wait_ge(t_out, f - 1)

        def t_fill(f, fs, src, k):
            t_wait(f)
            for j in range(2):
                for t in range(TT):
                    o = j * S + t * P
                    mm = pe.transpose(tr[fs % 2][:, o:o + P], src[:, t, (k + j) * P:(k + j + 1) * P], ident[:, :])
            mm.then_inc(t_filled, 1)

        def at_wait(f):
            if not (isinstance(f, int) and f < 2):
                pe.wait_ge(at_out, f - 1)

        pe.wait_ge(ident_ok, 1)
        pe.wait_ge(g_in, 16 * 7)
        pe.transpose(at[0][:, 0:NG], grow[:, :], ident[0:NG, 0:NG]).then_inc(at_filled, 1)
        pe.wait_ge(x_in[0], 16)
        t_fill(T_X, 0, bufX, 0)
        t_fill(T_X + 1, 1, bufX, 2)
        for v in range(16):
            if v < 6:
                if v == 2:
                    pe.wait_ge(x_in[1], 16)
                t_fill(T_X + v + 2, v, bufX, 2 * (v + 2))
            if v < 8:
                pe.wait_ge(t_out, T_X + v + 1)
            unit(V_LAT + v, v, lhsA, (2 * (v % 8), 2 * (v % 8) + 1), NC, U_LAT + v // 8, v % 8 == 0, v % 8 == 7)
            if v == 8:
                pe.wait_ge(c_in, 32)
                for j in range(4):
                    mm = pe.transpose(at[1][:, j * 2 * KF:(j + 1) * 2 * KF], crow[:, j, :], ident[0:2 * KF, 0:2 * KF])
                mm.then_inc(at_filled, 1)
            if v in (10, 12):
                pe.wait_ge(acc_out[0], U_LAT + 1)
                pe.wait_ge(acc_out[1], U_LAT + 1)
                t_fill(T_Q + (v - 10) // 2, (v - 10) // 2, zlat[:, 0, :, :], v - 10)
        for v in range(16):
            unit(V_POOLIN + v, v, lhsA, (2 * (v % 8), 2 * (v % 8) + 1), NC, U_POOLIN + v // 8, v % 8 == 0, v % 8 == 7)
            if v in (2, 4):
                pe.wait_ge(acc_out[0], U_LAT + 2)
                pe.wait_ge(acc_out[1], U_LAT + 2)
                t_fill(T_C + (v - 2) // 2, (v - 2) // 2, zlat[:, 1, :, :], v - 2)

        def pooled(f):
            t_wait(T_D + f)
            for j in range(2):
                k = 2 * f + j
                o = j * S
                pe.matmul(tr[f % 2][:, o:o + S], bufY[:, 0, k * P:(k + 1) * P], pm0[:, f, :], start=True, stop=False)
                mm = pe.matmul(tr[f % 2][:, o + P:o + S], bufY[:, 1, k * P:(k + 1) * P], pm1[:, f, :],
                               start=False, stop=True)
            mm.then_inc(t_filled, 1)

        pe.wait_ge(pm_ok, 8)
        for v in range(4):
            unit(V_KPE + v, v, lhsA, range(4 * v, 4 * v + 4), ROPE, U_KPE, v == 0, v == 3)
            if v == 0:
                for t in range(TT):
                    pe.wait_ge(acc_out[t], U_POOLIN + 2)
                pooled(0)
                pooled(1)
            if v == 2:
                pooled(2)
                pooled(3)
        for g in range(4):
            pe.wait_ge(lo_done, V_GRP + g + 1)
            pe.wait_ge(t_out, T_D + g + 1)
            t_wait(T_Y + g)
            s = (V_GRP + g) % AHEAD
            for j in range(2):
                dst = tr[g % 2][:, j * S:(j + 1) * S]
                for c in range(2):
                    o = c * 2 * P + j * P
                    wh, wl = whi[:, s, o:o + P], wlo[:, s, o:o + P]
                    dh, dl = lhsB(0, 2 * g + c), lhsB(1, 2 * g + c)
                    pe.matmul(dst, wh, dh, start=(c == 0), stop=False)
                    pe.matmul(dst, wl, dh, start=False, stop=False)
                    mm = pe.matmul(dst, wh, dl, start=False, stop=(c == 1))
            mm.then_inc(w_used, 1)
        pe.wait_ge(rope_ok, 1)
        for t in range(TT):
            mm = pe.transpose(at[A_KPE % 2][0:ROPE, t * P:(t + 1) * P], kpe[:, t, :], ident[:, :])
        mm.then_inc(at_filled, 1)
        pe.wait_ge(t_out, T_Y + 4)
        with pe.Fori(0, ND // 2) as i:
            for m in range(2):
                for k in range(4):
                    unit(V_YP + 8 * i + 4 * m + k, 4 * m + k,
                         lambda h, kt: lhsB(h, KP + kt), (2 * k, 2 * k + 1), NC, U_YP + 2 * i + m, k == 0, k == 3)
        with pe.Fori(0, NH // 4) as i:
            for m in range(2):
                v, u, f = V_ATT + 24 * i + 12 * m, U_ATT + 6 * i + 3 * m, A_PAIR + 10 * i + 5 * m
                pair, fs = 2 * i + m, A_PAIR + 5 * m
                for k in range(12):
                    if k < 2:
                        unit(v + k, k, lambda h, kt: lat[:, h, kt, :], (2 * k, 2 * k + 1), QPAIR, u, k == 0, k == 1)
                    elif k < 4:
                        unit(v + k, k, lambda h, kt: lat[:, h, KL + kt, :], (2 * k - 4, 2 * k - 3), NC, u + 1,
                             k == 2, k == 3)
                    else:
                        unit(v + k, k, lhsA, (2 * k - 8, 2 * k - 7), NC, u + 2, k == 4, k == 11)
                    if k in (5, 6):
                        h = k - 5
                        for t in range(TT):
                            pe.wait_ge(acc_out[t], u + 2)
                        at_wait(f + h)
                        if k == 6:
                            pe.wait_ge(rope_ok, pair + 2)
                            at_wait(f + 2)
                        for t in range(TT):
                            pe.transpose(at[(fs + h) % 2][:, t * P:(t + 1) * P],
                                         q_sb[:, t, h * (NOPE + ROPE):h * (NOPE + ROPE) + NOPE], ident[:, :])
                            mm = pe.transpose(at[(fs + h) % 2][:, S + t * P:S + (t + 1) * P],
                                              kv_sb[:, t, 2 * h * P:(2 * h + 1) * P], ident[:, :])
                        mm.then_inc(at_filled, 1)
                    if k == 6:
                        for h in range(2):
                            o = h * (NOPE + ROPE) + NOPE
                            for t in range(TT):
                                mm = pe.transpose(at[fs % 2][0:ROPE, h * S + t * P:h * S + (t + 1) * P],
                                                  q_sb[:, t, o:o + ROPE], ident[:, :])
                        mm.then_inc(at_filled, 1)
                    if k in (7, 8):
                        h = k - 7
                        pe.wait_ge(at_out, f + 3)
                        for t in range(TT):
                            w = (t + 1) * P
                            dst = sc[h][:, t * P:t * P + w]
                            pe.matmul(dst, qkT[:, h, t * P:(t + 1) * P], qkT[:, h, S:S + w], start=True, stop=False)
                            mm = pe.matmul(dst, qpeT[:, h, t * P:(t + 1) * P], kpeT[:, 0:w], start=False, stop=True)
                        mm.then_inc(s_filled, 1)
                    if k in (9, 10):
                        h = k - 9
                        pe.wait_ge(s_norm, 4 * pair + 2 * h + 2)
                        at_wait(f + 3 + h)
                        for b in range(3):
                            mm = pe.transpose(at[(fs + 3 + h) % 2][:, b * P:(b + 1) * P],
                                              prob[:, h, b * P:(b + 1) * P], ident[:, :])
                        mm.then_inc(at_filled, 1)
                    if k == 11:
                        pe.wait_ge(at_out, f + 5)
                        t_wait(T_O + pair)
                        for h in range(2):
                            vcol = slice((2 * h + 1) * P, (2 * h + 2) * P)
                            dst = tr[(T_O + m) % 2]
                            pe.matmul(dst[:, h * S:(h + 1) * S], kv_sb[:, 0, vcol], probT[:, h, 0:S],
                                      start=True, stop=False)
                            mm = pe.matmul(dst[:, h * S + P:(h + 1) * S], kv_sb[:, 1, vcol], probT[:, h, S:S + P],
                                           start=False, stop=True)
                        mm.then_inc(t_filled, 1)

        def column(v, u, lhs, job):
            for k in range(8):
                unit(v + k, k, lhs, (2 * k, 2 * k + 1), NC, u, k == 0, k == 7)
                job(k)

        def nothing(k):
            pass

        def merged(n):
            def job(k):
                if k in (2, 3):
                    pe.wait_ge(mrg_ok, 2 * n + 2)
                    t_fill(T_MRG + 2 * n + k - 2, k - 2, kch, 2 * (k - 2))
            return job

        def lhs_o(h, k):
            return actB[:, h, k, :]

        def ya_column(n, job):
            for k in range(8):
                if isinstance(n, int) and n == 0 and k == 6:
                    pe.wait_ge(t_out, T_O + 8)
                unit(V_YA + 8 * n + k, k, lhs_o, (2 * k, 2 * k + 1), NC, U_YA + n, k == 0, k == 7)
                job(k)

        pe.wait_ge(t_out, T_O + 7)
        ya_column(0, nothing)
        with pe.Fori(1, ND) as n:
            ya_column(n, merged(n - 1))

        for k in range(8):
            if k < 6 and k % 2 == 0:
                pe.wait_ge(t_out, T_MRG + k + 2)
            if k == 6:
                pe.wait_ge(t_out, T_MRG + 8)
            unit(V_MIX + k, k, lhsA, (2 * k, 2 * k + 1), NC, U_MIX, k == 0, k == 7)
            merged(ND - 1)(k)

        def mem_job(k):
            if k == 0:
                pe.wait_ge(mem_in, 16)
            t_fill(T_MEM + k, k, memv, 2 * k)

        column(V_MIX + 8, U_MIX + 1, lhsA, mem_job)
        with pe.Fori(2, ND) as n:
            column(V_MIX + 8 * n, U_MIX + n, lhsA, nothing)

        def mk_job(n):
            def job(k):
                if k == 1:
                    for t in range(TT):
                        pe.wait_ge(acc_out[t], U_MKV + n + 1)
                    for b in range(2):
                        at_wait(A_MK + 2 * n + b)
                        for j in range(2):
                            for t in range(TT):
                                mm = pe.transpose(at[(A_MK + b) % 2][:, j * S + t * P:j * S + (t + 1) * P],
                                                  kch[:, t, (2 * b + j) * P:(2 * b + j + 1) * P], ident[:, :])
                        mm.then_inc(at_filled, 1)
            return job

        pe.wait_ge(t_out, T_MEM + 8)
        column(V_MKV, U_MKV, lhsB, nothing)
        with pe.Fori(1, ND) as n:
            column(V_MKV + 8 * n, U_MKV + n, lhsB, mk_job(n - 1))

        def x2_job(k):
            pe.wait_ge(res_done, 8)
            t_fill(T_X2 + k, k, bufX, 2 * k)
            mk_job(ND - 1)(k)

        column(V_MKV + 8 * ND, U_MKV + ND, lhsB, x2_job)
        with pe.Fori(ND + 1, 2 * ND) as n:
            column(V_MKV + 8 * n, U_MKV + n, lhsB, nothing)

        def mem_head(n):
            def job(k):
                if k == 0:
                    for t in range(TT):
                        pe.wait_ge(acc_out[t], U_MQ + n + 1)
                    for b in range(2):
                        at_wait(A_MQ + 2 * n + b)
                        for j in range(2):
                            for t in range(TT):
                                mm = pe.transpose(at[(A_MQ + b) % 2][:, j * S + t * P:j * S + (t + 1) * P],
                                                  mq_sb[:, t, (2 * b + j) * P:(2 * b + j + 1) * P], ident[:, :])
                        mm.then_inc(at_filled, 1)
                if k == 1:
                    pe.wait_ge(at_out, A_MQ + 2 * n + 2)
                    for t in range(TT):
                        for d in range(4):
                            mm = pe.matmul(sc[0][:, t * S:(t + 1) * S], mqT[:, d, t * P:(t + 1) * P],
                                           memk[:, 4 * n + d, :], start=(d == 0), stop=(d == 3))
                    mm.then_inc(m_filled, 1)
                if k == 4:
                    pe.wait_ge(m_norm, 2 * n + 2)
                    for b in range(2):
                        for t in range(TT):
                            mm = pe.transpose(sc[1][:, b * S + t * P:b * S + (t + 1) * P],
                                              mp_sb[:, t, b * P:(b + 1) * P], ident[:, :])
                    mm.then_inc(mpT_filled, 1)
                if k in (5, 6):
                    pe.wait_ge(mpT_out, n + 1)
                    pe.wait_ge(mv_ok, n + 1)
                    t_wait(T_MOUT + 2 * n + k - 5)
                    for j in range(2):
                        d = 2 * (k - 5) + j
                        for b in range(2):
                            mm = pe.matmul(tr[(k - 5) % 2][:, j * S:(j + 1) * S], mv_sb[:, b, d * P:(d + 1) * P],
                                           mpT[:, b, :], start=(b == 0), stop=(b == 1))
                    mm.then_inc(t_filled, 1)
            return job

        pe.wait_ge(t_out, T_X2 + 8)
        column(V_MQ, U_MQ, lhsA, nothing)
        with pe.Fori(1, ND) as n:
            column(V_MQ + 8 * n, U_MQ + n, lhsA, mem_head(n - 1))
        pe.wait_ge(t_out, T_MOUT + 6)
        for k in range(8):
            if k == 6:
                mem_head(ND - 1)(6)
                pe.wait_ge(t_out, T_MOUT + 8)
            unit(V_MO + k, k, lhs_o, (2 * k, 2 * k + 1), NC, U_MO, k == 0, k == 7)
            if k != 6:
                mem_head(ND - 1)(k)
        with pe.Fori(1, ND) as n:
            column(V_MO + 8 * n, U_MO + n, lhs_o, nothing)

        def a_fill(m, i, banks, done):
            for t in range(TT):
                pe.wait_ge(acc_out[t], U_FIN + 2 * i + m + 1)
            if m == 1 or not isinstance(i, int) or i > 0:
                pe.wait_ge(gconv, 2 * i + 2 * m)
            for b in range(2):
                for j in range(2):
                    for t in range(TT):
                        mm = pe.transpose(banks[b][:, j * S + t * P:j * S + (t + 1) * P],
                                          a_sb[:, m, t, (2 * b + j) * P:(2 * b + j + 1) * P], ident[:, :])
                mm.then_inc(done, 1)

        def ffn_turn(i, first):
            for k in range(16):
                if first and k < 8:
                    if k < 6:
                        if k % 2 == 0:
                            pe.wait_ge(res_done, 8 + k + 4)
                        t_fill(T_X3 + k + 2, k, bufX, 2 * (k + 2))
                    pe.wait_ge(t_out, T_X3 + k + 1)
                unit(V_FIN + 16 * i + k, k, lhsA, (2 * (k % 8), 2 * (k % 8) + 1), NC, U_FIN + 2 * i + k // 8,
                     k % 8 == 0, k % 8 == 7)
                if k == 1 and not first:
                    a_fill(1, i - 1, at, ua_filled)
                if k == 9:
                    a_fill(0, i, sc, ga_filled)

        pe.wait_ge(res_done, 8 + 2)
        t_fill(T_X3, 0, bufX, 0)
        t_fill(T_X3 + 1, 1, bufX, 2)
        ffn_turn(0, True)
        with pe.Fori(1, NF) as i:
            ffn_turn(i, False)

        def lhsG(h, k):
            return gT[:, h, k, :]

        def fout(n, first):
            k0 = 0
            for k in range(24):
                kc = (2, 2, 2, 2, 2, 1)[k % 6]
                if first and k0 <= 4 * (NF - 1) < k0 + kc:
                    pe.wait_ge(f_lo, 2 * NF)
                unit(V_FOUT + 24 * n + k, k, lhsG, range(k0, k0 + kc), NC, U_FOUT + n, k == 0, k == 23)
                k0 += kc
                if first and k == 1:
                    a_fill(1, NF - 1, at, ua_filled)

        pe.wait_ge(f_lo, 2 * NF - 2)
        fout(0, True)
        with pe.Fori(1, ND) as n:
            fout(n, False)

    @block.scalar
    def _(act):
        def hi(v, vs):
            if isinstance(v, int) and v >= N_UNITS:
                return
            c = (vs // 2) % RAW_SLOTS
            turn = v // 8 if isinstance(v, int) else None
            act.wait_ge(w_loaded[c], 32 * (turn + 1))
            if v >= AHEAD:
                act.wait_ge(w_used, v - AHEAD + 1)
            w = width(v)
            act.activation(whi[:, vs % AHEAD, 0:w], raw[:, c, vs % 2, 0:w], ACT.Copy).then_inc(hi_done, 1)

        def hi_at(base, i, per, k):
            ks = base + k + AHEAD
            c = (ks // 2) % RAW_SLOTS
            if isinstance(i, int):
                v = ks + per * i
                if v < N_UNITS:
                    hi(v, v)
                return
            act.wait_ge(w_loaded[c], 32 * (ks // 8 + 1) + i * (4 * per))
            act.wait_ge(w_used, base + k + 1 + i * per)
            w = width(ks)
            act.activation(whi[:, ks % AHEAD, 0:w], raw[:, c, ks % 2, 0:w], ACT.Copy).then_inc(hi_done, 1)

        def evac(u, v, dst, n=None, width=NC, func=ACT.Copy):
            if n is not None:
                act.wait_ge(rstd_done, n + 1)
            for t in range(TT):
                if t == 0:
                    act.wait_ge(acc0_ready, u + 1)
                else:
                    act.wait_ge(w_used, v + 1)
                scale = 1.0 if n is None else rstd[:, n, t:t + 1]
                act.activation(dst[t], acc[t][:, 0:width], func, scale=scale).then_inc(acc_out[t], 1)

        def square(n, k, src, dst=None):
            j, t = k // 2, k % 2
            if SQ[n] + k > 0:
                act.wait_ge(sq_done, SQ[n] + k)
            act.activation(sc[0][:, :], src, ACT.Square,
                           accum_out=part[:, n, t, j:j + 1] if dst is None else dst).then_inc(sq_done, 1)

        def root(n):
            act.wait_ge(var_done, n + 1)
            act.activation(std[:, n, :], var[:, n, :], ACT.Sqrt).then_inc(std_done, 1)

        def t_split(f, fs, dst, scale=None, ready=None):
            if ready is None:
                act.wait_ge(t_filled, filled(f))
            else:
                act.wait_ge(w_used, ready)
            for j in range(2):
                act.activation(dst[j], tr[fs % 2][:, j * S:(j + 1) * S], ACT.Copy,
                               scale=1.0 if scale is None else gcol[:, scale + j:scale + j + 1]).then_inc(t_hi, 1)

        def at_copy(f, fs, dst, width=512, parts=P):
            act.wait_ge(at_filled, f + 1)
            act.activation(dst, at[fs % 2][0:parts, 0:width], ACT.Copy).then_inc(at_out, 1)

        act.dma_start(crow[:, 0:3, :], a["conv_w"][0].rearrange("c (f p) -> f c p", p=P)).then_inc(c_in, 16)
        act.dma_start(crow[:, 3, :], a["conv_b"][0].rearrange("(f p) -> f p", p=P)).then_inc(c_in, 16)
        act.dma_start(pos_i[:, :], a["positions"][0].rearrange("(t p) -> p t", p=P),
                      allow_slow_non_contiguous=True).then_inc(pos_in, 16)
        at_copy(A_SET, 0, gcol[:, :], NG)
        act.wait_ge(at_out, 1)
        for k in range(4):
            t_split(T_X + k, k, [actA[:, 0, 2 * k + j, :] for j in range(2)], G_MIX + 2 * k)
            hi(k, k)
        act.wait_ge(part_zero, 1)
        for k in range(16):
            if k < 4:
                t_split(T_X + k + 4, k, [actA[:, 0, 2 * k + 8 + j, :] for j in range(2)], G_MIX + 2 * k + 8)
            if k % 8 == 7:
                evac(U_LAT + k // 8, V_LAT + k, [zlat[:, k // 8, t, :] for t in range(TT)], N_X)
            hi_at(V_LAT, 0, 16, k)
            if k < 4:
                if k == 2:
                    act.wait_ge(x_in[1], 16)
                if k == 0:
                    act.wait_ge(x_in[0], 16)
                for t in range(TT):
                    square(N_X, 2 * k + t, bufX[:, t, k * NC:(k + 1) * NC])
            if k == 4:
                root(N_X)
            if k == 5:
                act.wait_ge(ang_ok, 1)
                act.activation(sinT[:, :, :], ang[:, :, :], ACT.Sin).then_inc(trig_ok, 1)
                act.activation(cosT[:, :, :], turns[:, :, :], ACT.Sin).then_inc(trig_ok, 1)
            if k % 8 == 7:
                for t in range(TT):
                    act.wait_ge(acc_out[t], U_LAT + k // 8 + 1)
                    square(N_Q + k // 8, t, zlat[:, k // 8, t, :])
            if k == 8:
                at_copy(A_SET + 1, 1, ccol[:, :, :].rearrange("p c f -> p (c f)"), 8 * KF)
                root(N_Q)
            if k in (10, 12):
                f = (k - 10) // 2
                t_split(T_Q + f, f, [lat[:, 0, 2 * f + j, :] for j in range(2)], G_Q + 2 * f)
        for k in range(16):
            if k % 8 == 7:
                evac(U_POOLIN + k // 8, V_POOLIN + k,
                     [bufY[:, t, k // 8 * NC:(k // 8 + 1) * NC] for t in range(TT)], N_X)
            hi_at(V_POOLIN, 0, 16, k)
            if k == 0:
                root(N_C)
            if k in (2, 4):
                f = (k - 2) // 2
                t_split(T_C + f, f, [lat[:, 0, KL + 2 * f + j, :] for j in range(2)], G_KV + 2 * f)
        for k in range(8):
            if k == 3:
                evac(U_KPE, V_KPE + 3, [kpe[:, t, :] for t in range(TT)], N_X, ROPE)
            hi_at(V_KPE, 0, 8, k)
            if k in (0, 2):
                for f in (k, k + 1):
                    t_split(T_D + f, f, [actB[:, 0, 2 * f + j, :] for j in range(2)])
            if k >= 4:
                g = k - 4
                t_split(T_Y + g, g, [actB[:, 0, KP + 2 * g + j, :] for j in range(2)], G_POOL + 2 * g,
                        V_GRP + g + 1)
        at_copy(A_KPE, A_KPE, kpeT[:, :], S, ROPE)
        with act.Fori(0, ND // 2) as i:
            for m in range(2):
                for k in range(4):
                    if k == 3:
                        evac(U_YP + 2 * i + m, V_YP + 8 * i + 4 * m + 3,
                             [bufY[:, t, bass.ds(i * 2 * NC + m * NC, NC)] for t in range(TT)])
                    hi_at(V_YP, i, 8, 4 * m + k)
        with act.Fori(0, NH // 4) as i:
            for m in range(2):
                v, u, f = V_ATT + 24 * i + 12 * m, U_ATT + 6 * i + 3 * m, A_PAIR + 10 * i + 5 * m
                pair, fs = 2 * i + m, A_PAIR + 5 * m
                for k in range(12):
                    if k == 1:
                        evac(u, v + 1, [q_sb[:, t, :] for t in range(TT)], N_Q, QPAIR)
                    if k == 3:
                        evac(u + 1, v + 3, [kv_sb[:, t, :] for t in range(TT)], N_C)
                    if k == 11 and m == 0:
                        evac(u + 2, v + 11, [bufX[:, t, bass.ds(i * NC, NC)] for t in range(TT)], N_X,
                             func=ACT.Sigmoid)
                    if k == 11 and m == 1:
                        act.wait_ge(mp_ok, 2 * i + 1)
                        evac(u + 2, v + 11, [gp_sb[:, t, :] for t in range(TT)], N_X, func=ACT.Sigmoid)
                    hi_at(V_ATT, i, 24, 12 * m + k)
                    if k == 5:
                        at_copy(f, fs, qkT[:, 0, :])
                    if k == 6:
                        at_copy(f + 1, fs + 1, qkT[:, 1, :])
                        at_copy(f + 2, fs, qpeT[:, :, :].rearrange("p h s -> p (h s)"), 512, ROPE)
                    if k in (8, 9):
                        h = k - 8
                        act.wait_ge(s_nmax, 2 * pair + h + 1)
                        for t in range(TT):
                            pr = prob[:, h, t * P:(2 * t + 1) * P]
                            act.activation(pr, pr, ACT.Exp, bias=nmax[:, h, t:t + 1], scale=SCALE,
                                           accum_out=ssum[:, h, t:t + 1]).then_inc(s_exp, 1)
                    if k in (9, 10):
                        at_copy(f + k - 6, fs + k - 6, probT[:, k - 9, :], 3 * P)
                    if k == 11:
                        t_split(T_O + pair, T_O + m, [actB[:, 0, 4 * i + 2 * m + j, :] for j in range(2)])

        def merged(n):
            def job(k):
                if k in (2, 3):
                    t_split(T_MRG + 2 * n + k - 2, k - 2, [actA[:, 0, 4 * n + 2 * (k - 2) + j, :] for j in range(2)])
            return job

        def nothing(k):
            pass

        def column(base, u, n, i_dst, norm, job, y=None):
            for k in range(8):
                if k == 7:
                    evac(u + n, base + 8 * n + 7, i_dst, norm)
                if k == 7 and y is not None:
                    for t in range(TT):
                        act.wait_ge(acc_out[t], u + n + 1)
                        act.wait_ge(sq_done, SQ[y] + 2 * n + t)
                        act.activation(sc[0][:, :], i_dst[t], ACT.Square,
                                       accum_out=part[:, y, t, bass.ds(n, 1)]).then_inc(sq_done, 1)
                hi_at(base, n, 8, k)
                job(k)

        def chunk(buf, n):
            return [buf[:, t, bass.ds(n * NC, NC)] for t in range(TT)]

        kch_t = [kch[:, t, :] for t in range(TT)]
        act.wait_ge(mp_ok, 2 * ND + 1)
        column(V_YA, U_YA, 0, kch_t, None, nothing)
        act.wait_ge(t_out, T_O + 8)
        act.dma_start(memv[:, :, :], memtok).then_inc(mem_in, 16)
        with act.Fori(1, ND) as n:
            column(V_YA, U_YA, n, kch_t, None, merged(n - 1))

        def mem_squares(k):
            if k == 0:
                act.wait_ge(mem_in, 16)
            for q in (k,) if k < 6 else (6, 7) if k == 6 else ():
                square(N_MEM, q, memv[:, q % 2, q // 2 * NC:(q // 2 + 1) * NC])
            merged(ND - 1)(k)
            if k == 2:
                act.wait_ge(mrg_ok, 2 * ND)
                act.dma_start(bufX[:, :, :], tok).then_inc(x_again, 16)

        column(V_MIX, U_MIX, 0, chunk(bufY, 0), None, mem_squares, y=N_Y1)

        def mem_split(k):
            if k == 0:
                root(N_MEM)
            t_split(T_MEM + k, k, [actB[:, 0, 2 * k + j, :] for j in range(2)], G_MEMKV + 2 * k)
            if k == 7:
                act.dma_start(gpost, a["g_mix_post"].broadcast_to([P, D])).then_inc(gpost_in, 16)

        column(V_MIX, U_MIX, 1, chunk(bufY, 1), None, mem_split, y=N_Y1)
        with act.Fori(2, ND) as n:
            column(V_MIX, U_MIX, n, chunk(bufY, n), None, nothing, y=N_Y1)

        def x2_squares(k):
            if k == 0:
                root(N_Y1)
            for q in ([] if k == 0 else [k - 1] if k < 7 else [6, 7]):
                act.wait_ge(res_done, q + 1)
                square(N_X2, q, bufX[:, q % 2, q // 2 * NC:(q // 2 + 1) * NC])

        def mk_job(n):
            def job(k):
                if k == 1:
                    for b in range(2):
                        at_copy(A_MK + 2 * n + b, A_MK + b,
                                memk[:, bass.ds(4 * n + 2 * b, 2), :].rearrange("p k s -> p (k s)"))
            return job

        column(V_MKV, U_MKV, 0, kch_t, N_MEM, x2_squares)
        with act.Fori(1, ND) as n:
            column(V_MKV, U_MKV, n, kch_t, N_MEM, mk_job(n - 1))

        def x2_split(k):
            if k == 0:
                root(N_X2)
            t_split(T_X2 + k, k, [actA[:, 0, 2 * k + j, :] for j in range(2)], G_MEM + 2 * k)
            mk_job(ND - 1)(k)

        column(V_MKV, U_MKV, ND, chunk(memv, 0), N_MEM, x2_split)
        with act.Fori(ND + 1, 2 * ND) as n:
            column(V_MKV, U_MKV, n, chunk(memv, n - ND), N_MEM, nothing)

        def mem_head(n):
            def job(k):
                if k == 0:
                    for b in range(2):
                        at_copy(A_MQ + 2 * n + b, A_MQ + b, mqT[:, 2 * b:2 * b + 2, :].rearrange("p k s -> p (k s)"))
                if k == 2:
                    act.wait_ge(m_nmax, n + 1)
                    for t in range(TT):
                        act.activation(mp_sb[:, t, :], sc[0][:, t * S:(t + 1) * S], ACT.Exp, bias=mnmax[:, t:t + 1],
                                       scale=MSCALE, accum_out=msum[:, t:t + 1]).then_inc(m_exp, 1)
                if k == 4:
                    act.wait_ge(mpT_filled, n + 1)
                    act.activation(mpT, sc[1][:, :].rearrange("p (b s) -> p b s", b=2), ACT.Copy).then_inc(mpT_out, 1)
                if k in (5, 6):
                    t_split(T_MOUT + 2 * n + k - 5, k - 5,
                            [actB[:, 0, 4 * n + 2 * (k - 5) + j, :] for j in range(2)])
            return job

        mq_t = [mq_sb[:, t, :] for t in range(TT)]
        column(V_MQ, U_MQ, 0, mq_t, N_X2, nothing)
        with act.Fori(1, ND) as n:
            column(V_MQ, U_MQ, n, mq_t, N_X2, mem_head(n - 1))

        def last_head(k):
            if k == 5:
                mem_head(ND - 1)(5)
                mem_head(ND - 1)(6)
                act.wait_ge(mv_ok, ND)
                act.dma_start(gpost, a["g_mem_post"].broadcast_to([P, D])).then_inc(gpost_in, 16)
            elif k != 6:
                mem_head(ND - 1)(k)

        column(V_MO, U_MO, 0, chunk(bufY, 0), None, last_head, y=N_Y2)
        with act.Fori(1, ND) as n:
            column(V_MO, U_MO, n, chunk(bufY, n), None, nothing, y=N_Y2)

        def up_hi(i, b):
            act.wait_ge(f_mul, 2 * i + b + 1)
            act.activation(gT[:, 0, bass.ds(4 * i + 2 * b, 2), :], cu[:, 2 * b:2 * b + 2, :], ACT.Copy).then_inc(f_hi, 1)

        def ffn_turn(i, first):
            for k in range(16):
                if first and k < 8:
                    t_split(T_X3 + k, k, [actA[:, 0, 2 * k + j, :] for j in range(2)], G_FFN + 2 * k)
                    if k % 2 == 0:
                        for t in range(TT):
                            act.wait_ge(res_done, 8 + k + t + 1)
                            square(N_X3, k + t, bufX[:, t, k // 2 * NC:(k // 2 + 1) * NC])
                    if k == 7:
                        root(N_X3)
                        act.wait_ge(res_done, 16)
                        act.dma_start(x3_spill.rearrange("(t p) d -> p t d", p=P), bufX[:, :, :]).then_inc(spill, 16)
                if k % 8 == 7:
                    m = k // 8
                    evac(U_FIN + 2 * i + m, V_FIN + 16 * i + k, [a_sb[:, m, t, :] for t in range(TT)], N_X3)
                hi_at(V_FIN, i, 16, k)
                if not first and k in (3, 5):
                    up_hi(i - 1, k // 4)
                if k == 13:
                    act.wait_ge(gconv, 2 * i + 2)
                    g = cg[:, :, :].rearrange("p f s -> p (f s)")
                    act.activation(g, g, ACT.Gelu_apprx_tanh).then_inc(gelu_ok, 1)

        root(N_Y2)
        ffn_turn(0, True)
        act.wait_ge(spill, 16)
        with act.Fori(1, NF) as i:
            ffn_turn(i, False)

        def fout(n, first):
            for k in range(24):
                if k == 23:
                    evac(U_FOUT + n, V_FOUT + 24 * n + 23, chunk(y3, n))
                if not (isinstance(n, int) and n == ND - 1 and k >= 20):
                    hi_at(V_FOUT, n, 24, k)
                if first and k == 0:
                    act.wait_ge(w_used, V_FOUT)
                    act.dma_start(x3[:, :, :], x3_spill.rearrange("(t p) d -> p t d", p=P)).then_inc(x3_in, 16)
                if first and k in (3, 5):
                    up_hi(NF - 1, k // 4)
                if first and k == 6:
                    act.wait_ge(ua_filled, 2 * NF)
                    act.dma_start(gpost3, a["g_ffn_post"].broadcast_to([P, D])).then_inc(gpost_in, 16)
                if k == 23:
                    for t in range(TT):
                        act.wait_ge(acc_out[t], U_FOUT + n + 1)
                        act.wait_ge(sq_done, SQ[N_Y3] + 2 * n + t)
                        act.activation(sc[0][:, :], chunk(y3, n)[t], ACT.Square,
                                       accum_out=part[:, N_Y3, t, bass.ds(n, 1)]).then_inc(sq_done, 1)

        fout(0, True)
        with act.Fori(1, ND - 1) as n:
            fout(n, False)
        fout(ND - 1, False)
        root(N_Y3)

    @block.vector
    def _(dve):
        def lo(v, vs):
            c, w = (vs // 2) % RAW_SLOTS, width(vs)
            dve.wait_ge(hi_done, v + 1)
            dve.tensor_tensor(wlo[:, vs % AHEAD, 0:w], raw[:, c, vs % 2, 0:w], f32(whi[:, vs % AHEAD, 0:w]),
                              ALU.subtract).then_inc(lo_done, 1)

        def lo_at(base, i, per, k):
            v = base + k + AHEAD + i * per
            if isinstance(v, int) and v >= N_UNITS:
                return
            lo(v, base + k + AHEAD if not isinstance(v, int) else v)

        def t_split(f, fs, hi_, lo_, scale=None):
            dve.wait_ge(t_hi, 2 * f + 2)
            for j in range(2):
                src = tr[fs % 2][:, j * S:(j + 1) * S]
                if scale is None:
                    op = dve.tensor_tensor(lo_[j], src, f32(hi_[j]), ALU.subtract)
                else:
                    op = dve.scalar_tensor_tensor(out=lo_[j], in0=src, scalar=gcol[:, scale + j:scale + j + 1],
                                                  in1=f32(hi_[j]), op0=ALU.mult, op1=ALU.subtract)
            op.then_inc(t_out, 1)

        def tiles(buf, k):
            return [[buf[:, h, k + j, :] for j in range(2)] for h in range(2)]

        def norm(n, parts, width=D):
            dve.wait_ge(sq_done, SQ[n] + parts)
            dve.tensor_reduce(ssq[:, n, :], part[:, n, :, :], AX.X, ALU.add).then_inc(sum_done, 1)
            dve.wait_ge(sum_done, n + 1)
            dve.tensor_scalar(var[:, n, :], ssq[:, n, :], 1.0 / width, EPS, ALU.mult, ALU.add).then_inc(var_done, 1)
            dve.wait_ge(std_done, n + 1)
            dve.reciprocal(rstd[:, n, :], std[:, n, :]).then_inc(rstd_done, 1)

        steps = [0]

        def step(op):
            op.then_inc(rope_step, 1)
            steps[0] += 1
            dve.wait_ge(rope_step, steps[0])

        def rotate(xs, first_step, rotations):
            if not isinstance(rotations, int):
                dve.wait_ge(rope_ok, rotations)
            for h, x in enumerate(xs):
                x1, x2 = x[:, :, 0:HALF], x[:, :, HALF:ROPE]
                dve.tensor_tensor(rope_part(h, 0), x1, cosT[:, :, :], ALU.mult)
                dve.tensor_tensor(rope_part(h, 1), x2, sinT[:, :, :], ALU.mult)
                dve.tensor_tensor(rope_part(h, 2), x2, cosT[:, :, :], ALU.mult)
                last = dve.tensor_tensor(rope_part(h, 3), x1, sinT[:, :, :], ALU.mult)
            last.then_inc(rope_step, 1)
            dve.wait_ge(rope_step, first_step + 1)
            for h, x in enumerate(xs):
                dve.tensor_tensor(x[:, :, 0:HALF], rope_part(h, 0), rope_part(h, 1), ALU.subtract)
                last = dve.tensor_tensor(x[:, :, HALF:ROPE], rope_part(h, 2), rope_part(h, 3), ALU.add)
            last.then_inc(rope_ok, 1)

        def rope_part(h, j):
            return ropet[:, j, h * TT * HALF:(h + 1) * TT * HALF].rearrange("p (t c) -> p t c", t=TT)

        dve.memset(part[:, :, :, :], 0.0).then_inc(part_zero, 1)
        dve.wait_ge(at_out, 1)
        for k in range(4):
            t_split(T_X + k, k, *tiles(actA, 2 * k), G_MIX + 2 * k)
            lo(k, k)
        for k in range(16):
            if k < 4:
                t_split(T_X + k + 4, k, *tiles(actA, 2 * k + 8), G_MIX + 2 * k + 8)
            lo_at(V_LAT, 0, 16, k)
            if k == 3:
                dve.wait_ge(pos_in, 16)
                dve.wait_ge(consts_ok, 1)
                step(dve.tensor_copy(posf[:, :], pos_i[:, :]))
                for t in range(TT):
                    step(dve.tensor_scalar(ang[:, t, :], invf[:, :], posf[:, t:t + 1], None, ALU.mult))
                step(dve.tensor_scalar(turns[:, :, :], ang[:, :, :], float(1 / (2 * np.pi)), ROUND, ALU.mult, ALU.add))
                step(dve.tensor_scalar(turns[:, :, :], turns[:, :, :], ROUND, None, ALU.subtract))
                for c in (TWO_PI_A, TWO_PI_B, TWO_PI_C):
                    step(dve.scalar_tensor_tensor(out=ang[:, :, :], in0=turns[:, :, :], scalar=-c,
                                                  in1=ang[:, :, :], op0=ALU.mult, op1=ALU.add))
                step(dve.tensor_scalar(ang[:, :, :], ang[:, :, :], 3.1415925, -3.1415925, ALU.min, ALU.max))
                step(dve.scalar_tensor_tensor(out=turns[:, :, :], in0=ang[:, :, :], scalar=-1.0, in1=ang[:, :, :],
                                              op0=ALU.mult, op1=ALU.min))
                dve.tensor_scalar(turns[:, :, :], turns[:, :, :], float(np.pi / 2), None, ALU.add).then_inc(ang_ok, 1)
            if k == 4:
                norm(N_X, 8)
            if k == 8:
                norm(N_Q, 2, QL)
            if k in (10, 12):
                t_split(T_Q + (k - 10) // 2, (k - 10) // 2, *tiles(lat, k - 10), G_Q + k - 10)
        for k in range(16):
            lo_at(V_POOLIN, 0, 16, k)
            if k == 0:
                norm(N_C, 2, QL)
            if k in (2, 4):
                t_split(T_C + (k - 2) // 2, (k - 2) // 2, *tiles(lat, KL + k - 2), G_KV + k - 2)
        for k in range(8):
            lo_at(V_KPE, 0, 8, k)
            if k in (0, 2):
                for f in (k, k + 1):
                    t_split(T_D + f, f, *tiles(actB, 2 * f))
            if k == 3:
                dve.wait_ge(trig_ok, 2)
                for t in range(TT):
                    dve.wait_ge(acc_out[t], U_KPE + 1)
                rotate([kpe[:, :, :]], steps[0], 0)
                steps[0] += 1
            if k >= 4:
                t_split(T_Y + k - 4, k - 4, *tiles(actB, KP + 2 * (k - 4)), G_POOL + 2 * (k - 4))
        with dve.Fori(0, ND // 2) as i:
            for k in range(8):
                lo_at(V_YP, i, 8, k)
        dve.wait_ge(consts_ok, 3)
        with dve.Fori(0, NH // 4) as i:
            for m in range(2):
                u, pair = U_ATT + 6 * i + 3 * m, 2 * i + m

                def row_max(h):
                    n = 2 * pair + h
                    dve.wait_ge(s_filled, n + 1)
                    dve.tensor_tensor(prob[:, h, 0:P], sc[h][:, 0:P], mask[:, 0:P], ALU.add).then_inc(s_max, 1)
                    dve.tensor_tensor_reduce(prob[:, h, P:3 * P], sc[h][:, P:3 * P], mask[:, P:3 * P], 1.0, -3.0e38,
                                             ALU.add, ALU.max, smax[:, h, 1:2]).then_inc(s_max, 1)
                    dve.wait_ge(s_max, 3 * n + 1)
                    dve.tensor_reduce(smax[:, h, 0:1], prob[:, h, 0:P], AX.X, ALU.max).then_inc(s_max, 1)
                    dve.wait_ge(s_max, 3 * n + 3)
                    dve.tensor_scalar(nmax[:, h, :], smax[:, h, :], -SCALE, None, ALU.mult).then_inc(s_nmax, 1)

                def normalise(h):
                    n = 2 * pair + h
                    dve.wait_ge(s_exp, 2 * n + 2)
                    dve.reciprocal(rsum[:, h, :], ssum[:, h, :]).then_inc(s_rsum, 1)
                    dve.wait_ge(s_rsum, n + 1)
                    for t in range(TT):
                        o = slice(t * P, (2 * t + 1) * P)
                        dve.tensor_scalar(prob[:, h, o], prob[:, h, o], rsum[:, h, t:t + 1], None,
                                          ALU.mult).then_inc(s_norm, 1)

                for k in range(12):
                    lo_at(V_ATT, i, 24, 12 * m + k)
                    if k == 3:
                        for t in range(TT):
                            dve.wait_ge(acc_out[t], u + 1)
                        rotate([q_sb[:, :, o:o + ROPE] for o in (NOPE, 2 * NOPE + ROPE)], steps[0] + pair, pair + 1)
                    if k == 7:
                        row_max(0)
                    if k == 8:
                        row_max(1)
                        normalise(0)
                    if k == 9:
                        normalise(1)
                    if k == 11:
                        t_split(T_O + pair, T_O + m, *tiles(actB, 4 * i + 2 * m))

        def column(base, n, job):
            for k in range(8):
                lo_at(base, n, 8, k)
                job(k)

        def nothing(k):
            pass

        def merge(n):
            def job(k):
                if k == 0:
                    for t in range(TT):
                        dve.wait_ge(acc_out[t], U_YA + n + 1)
                        dve.wait_ge(mp_ok, 2 * ND + 1)
                        y, g, b = (kch[:, t, :], bufX[:, t, bass.ds(n * NC, NC)], bufY[:, t, bass.ds(n * NC, NC)])
                        dve.tensor_tensor(y, y, g, ALU.mult).then_inc(mrg_mul, 1)
                        dve.wait_ge(mrg_mul, 2 * n + t + 1)
                        dve.tensor_tensor(y, y, b, ALU.add).then_inc(mrg_ok, 1)
                if k in (2, 3):
                    t_split(T_MRG + 2 * n + k - 2, k - 2, *tiles(actA, 4 * n + 2 * (k - 2)))
            return job

        column(V_YA, 0, nothing)
        with dve.Fori(1, ND) as n:
            column(V_YA, n, merge(n - 1))
        column(V_MIX, 0, merge(ND - 1))

        def mem_split(k):
            if k == 0:
                norm(N_MEM, 8)
            t_split(T_MEM + k, k, *tiles(actB, 2 * k), G_MEMKV + 2 * k)

        column(V_MIX, 1, mem_split)
        with dve.Fori(2, ND) as n:
            column(V_MIX, n, nothing)

        def residual(n, r, q, y, x, dst, gained):
            t, o = q % 2, slice(q // 2 * NC, (q // 2 + 1) * NC)
            dve.wait_ge(y_gained, gained + q + 1)
            dve.scalar_tensor_tensor(out=dst[:, t, o], in0=y[:, t, o], scalar=rstd[:, n, t:t + 1], in1=x[:, t, o],
                                     op0=ALU.mult, op1=ALU.add).then_inc(res_done, 1)

        def x2_job(k):
            if k == 0:
                norm(N_Y1, 8)
                dve.wait_ge(rstd_done, N_Y1 + 1)
                dve.wait_ge(x_again, 16)
            residual(N_Y1, 0, k, bufY, bufX, bufX, 0)

        column(V_MKV, 0, x2_job)
        with dve.Fori(1, ND) as n:
            column(V_MKV, n, nothing)

        def x2_split(k):
            if k == 0:
                norm(N_X2, 8)
            t_split(T_X2 + k, k, *tiles(actA, 2 * k), G_MEM + 2 * k)

        column(V_MKV, ND, x2_split)
        with dve.Fori(ND + 1, 2 * ND) as n:
            column(V_MKV, n, nothing)

        def mem_head(n):
            def job(k):
                if k == 1:
                    dve.wait_ge(m_filled, n + 1)
                    dve.tensor_reduce(mmax[:, :], sc[0][:, :].rearrange("p (t s) -> p t s", t=TT), AX.X,
                                      ALU.max).then_inc(m_max, 1)
                    dve.wait_ge(m_max, n + 1)
                    dve.tensor_scalar(mnmax[:, :], mmax[:, :], -MSCALE, None, ALU.mult).then_inc(m_nmax, 1)
                if k == 3:
                    dve.wait_ge(m_exp, 2 * n + 2)
                    dve.reciprocal(mrsum[:, :], msum[:, :]).then_inc(m_rsum, 1)
                    dve.wait_ge(m_rsum, n + 1)
                    for t in range(TT):
                        dve.tensor_scalar(mp_sb[:, t, :], mp_sb[:, t, :], mrsum[:, t:t + 1], None,
                                          ALU.mult).then_inc(m_norm, 1)
                if k in (5, 6):
                    t_split(T_MOUT + 2 * n + k - 5, k - 5, *tiles(actB, 4 * n + 2 * (k - 5)))
            return job

        column(V_MQ, 0, nothing)
        with dve.Fori(1, ND) as n:
            column(V_MQ, n, mem_head(n - 1))

        def last_head(k):
            if k == 5:
                mem_head(ND - 1)(5)
                mem_head(ND - 1)(6)
            elif k != 6:
                mem_head(ND - 1)(k)

        column(V_MO, 0, last_head)
        with dve.Fori(1, ND) as n:
            column(V_MO, n, nothing)

        def conv(src, dst, col, first_step, done):
            tile = [(src[:, j * S:(j + 1) * S], dst[:, j, :],
                     [ccol[:, c, bass.ds(col + j, 1)] for c in range(4)]) for j in range(2)]
            for x, y, w in tile:
                dve.tensor_scalar(y, x, w[2], w[3], ALU.mult, ALU.add).then_inc(conv_step, 1)
            for j, (x, y, w) in enumerate(tile):
                dve.wait_ge(conv_step, first_step + j + 1)
                dve.scalar_tensor_tensor(out=y[:, 1:S], in0=x[:, 0:S - 1], scalar=w[1], in1=y[:, 1:S],
                                         op0=ALU.mult, op1=ALU.add).then_inc(conv_step, 1)
            for j, (x, y, w) in enumerate(tile):
                dve.wait_ge(conv_step, first_step + j + 3)
                last = dve.scalar_tensor_tensor(out=y[:, 2:S], in0=x[:, 0:S - 2], scalar=w[0], in1=y[:, 2:S],
                                                op0=ALU.mult, op1=ALU.add)
            last.then_inc(done, 1)

        def up_conv(i, b):
            u = cu[:, 2 * b:2 * b + 2, :]
            dve.wait_ge(ua_filled, 2 * i + b + 1)
            dve.wait_ge(gelu_ok, i + 1)
            conv(at[b], u, 4 * i + KF + 2 * b, 16 * i + 8 + 4 * b, uconv)
            dve.wait_ge(uconv, 2 * i + b + 1)
            dve.tensor_tensor(u, u, cg[:, 2 * b:2 * b + 2, :], ALU.mult).then_inc(f_mul, 1)

        def up_lo(i, b):
            dve.wait_ge(f_hi, 2 * i + b + 1)
            g = [gT[:, h, bass.ds(4 * i + 2 * b, 2), :] for h in range(2)]
            dve.tensor_tensor(g[1], cu[:, 2 * b:2 * b + 2, :], f32(g[0]), ALU.subtract).then_inc(f_lo, 1)

        def up_job(i, k):
            if k in (1, 3):
                up_conv(i, k // 2)
            if k in (4, 6):
                up_lo(i, k // 2 - 2)

        def ffn_turn(i, first):
            for k in range(16):
                if first and k < 8:
                    t_split(T_X3 + k, k, *tiles(actA, 2 * k), G_FFN + 2 * k)
                    if k in (0, 2, 4):
                        residual(N_Y2, 0, k + 2, bufY, bufX, bufX, 8)
                        residual(N_Y2, 0, k + 3, bufY, bufX, bufX, 8)
                lo_at(V_FIN, i, 16, k)
                if first and k == 6:
                    norm(N_X3, 8)
                if not first:
                    up_job(i - 1, k)
                if k in (9, 11):
                    b = k // 2 - 4
                    dve.wait_ge(ga_filled, 2 * i + b + 1)
                    conv(sc[b], cg[:, 2 * b:2 * b + 2, :], 4 * i + 2 * b, 16 * i + 4 * b, gconv)

        norm(N_Y2, 8)
        dve.wait_ge(rstd_done, N_Y2 + 1)
        residual(N_Y2, 0, 0, bufY, bufX, bufX, 8)
        residual(N_Y2, 0, 1, bufY, bufX, bufX, 8)
        ffn_turn(0, True)
        with dve.Fori(1, NF) as i:
            ffn_turn(i, False)

        def fout(n, first):
            for k in range(24):
                if not (isinstance(n, int) and n == ND - 1 and k >= 20):
                    lo_at(V_FOUT, n, 24, k)
                if first:
                    up_job(NF - 1, k)

        fout(0, True)
        with dve.Fori(1, ND - 1) as n:
            fout(n, False)
        fout(ND - 1, False)
        norm(N_Y3, 8)
        dve.wait_ge(rstd_done, N_Y3 + 1)
        dve.wait_ge(x3_in, 16)
        for q in range(8):
            residual(N_Y3, 0, q, y3, x3, y3, 16)

    ctx.close()


_INS = ["x", "mem", "positions", "g_mix_pre", "w_in", "g_q_a", "w_q_b", "g_kv_a", "w_kv_b", "w_attn_br",
        "w_pool_grp", "pool_scale", "w_pool_br", "w_mix_out", "g_mix_post", "g_mem_pre", "g_mem_kv", "w_mem_q",
        "w_mem_kv", "w_mem_o", "g_mem_post", "g_ffn_pre", "w_ffn_in", "conv_w", "conv_b", "w_ffn_out", "g_ffn_post"]


def kernel(**inputs):
    import concourse.bacc as _bacc
    from concourse.bass_utils import run_bass_kernel_spmd as _run

    nc = _bacc.Bacc("TRN2", target_bir_lowering=False, num_devices=1)
    arrays, aps = {}, {}
    for name in _INS:
        v = np.ascontiguousarray(inputs[name])
        arrays[f"in_{name}"] = v
        aps[name] = nc.dram_tensor(f"in_{name}", v.shape, mybir.dt.from_np(v.dtype), kind="ExternalInput").ap()
    shape = inputs["x"].shape
    out = nc.dram_tensor("out_x", shape, F32, kind="ExternalOutput").ap()
    spill = nc.dram_tensor("x3_spill", shape[1:], F32, kind="Internal").ap()
    hybrid_layer(nc, aps, out, spill)
    r = _run(nc, [arrays], core_ids=[0])
    return r.results[0]["out_x"]
```

```python
from contextlib import ExitStack

import numpy as np

import concourse.bass as bass
from concourse import mybir

ALU = mybir.AluOpType
ACT = mybir.ActivationFunctionType
AX = mybir.AxisListType
F32 = mybir.dt.float32
F32R = mybir.dt.float32r
I32 = mybir.dt.int32

P = 128
NEG = -1.0e30
THETA = 10000.0
EPS = 1e-6
WINDOWS = (2, 4, 8, 16)
RAW_SLOTS = 4
AHEAD = 4
WARM_UP = 12
TWO_PI_A = 6.28125
TWO_PI_B = 0.0019350051879882812
TWO_PI_C = float(2 * np.pi - TWO_PI_A - TWO_PI_B)
ROUND = 12582912.0


def hybrid_layer(nc, a, out, x3_spill):
    S, D = a["x"].shape[1:]
    TT = S // P
    KD = D // P
    QL = a["w_q_b"].shape[1]
    KL = QL // P
    NH = 16
    NOPE, ROPE, VD = 128, 64, 128
    HALF = ROPE // 2
    PW = a["w_pool_br"].shape[1]
    KP = PW // P
    DFF = a["w_ffn_out"].shape[1]
    KF = DFF // P
    NC = 512
    ND = D // NC
    NF = DFF // NC
    QPAIR = 2 * (NOPE + ROPE)
    SCALE = float((NOPE + ROPE) ** -0.5)
    MHD = D // 4
    MSCALE = float(MHD ** -0.5)

    V_LAT = 0
    V_POOLIN = V_LAT + 2 * KD // 2
    V_KPE = V_POOLIN + 2 * KD // 2
    V_GRP = V_KPE + 4
    V_YP = V_GRP + 4
    V_ATT = V_YP + ND * KP // 2
    V_YA = V_ATT + NH // 2 * 12
    V_MIX = V_YA + ND * 8
    V_MKV = V_MIX + ND * 8
    V_MQ = V_MKV + 2 * ND * 8
    V_MO = V_MQ + ND * 8
    V_FIN = V_MO + ND * 8
    V_FOUT = V_FIN + 2 * NF * 8
    N_UNITS = V_FOUT + ND * 24

    U_LAT, U_POOLIN, U_KPE, U_YP, U_ATT = 0, 2, 4, 5, 9
    U_YA = U_ATT + 3 * NH // 2
    U_MIX = U_YA + ND
    U_MKV = U_MIX + ND
    U_MQ = U_MKV + 2 * ND
    U_MO = U_MQ + ND
    U_FIN = U_MO + ND
    U_FOUT = U_FIN + 2 * NF

    T_X, T_Q, T_C, T_D, T_Y, T_O = 0, 8, 10, 12, 16, 20
    T_MRG = T_O + NH // 2
    T_MEM = T_MRG + 8
    T_X2 = T_MEM + 8
    T_MOUT = T_X2 + 8
    T_X3 = T_MOUT + 8

    A_SET, A_KPE, A_PAIR = 0, 2, 3
    A_MK = A_PAIR + 5 * NH // 2
    A_MQ = A_MK + 2 * ND

    N_X, N_Q, N_C, N_MEM, N_Y1, N_X2, N_Y2, N_X3, N_Y3 = range(9)

    G_MEM, G_MEMKV, G_FFN = 0, KD, 2 * KD
    G_Q, G_KV, G_POOL = 3 * KD, 3 * KD + KL, 3 * KD + 2 * KL
    NG = 3 * KD + 2 * KL + KP

    def rows(name):
        return a[name][0].rearrange("(k p) n -> p k n", p=P)

    w_in, w_qb, w_kvb = rows("w_in"), rows("w_q_b"), rows("w_kv_b")
    w_grp = a["w_pool_grp"][0].rearrange("g (c p) d -> p (g c) d", p=P)
    C_Q, C_C, C_PE, C_U = 0, QL, 2 * QL, 2 * QL + ROPE
    C_GA, C_GP = C_U + PW, C_U + PW + D
    tok = a["x"][0].rearrange("(t p) d -> p t d", p=P)
    memtok = a["mem"][0].rearrange("(t p) d -> p t d", p=P)
    outtok = out[0].rearrange("(t p) d -> p t d", p=P)

    ctx = ExitStack()

    def sb(scope, name, shape, dt=F32):
        return scope.enter_context(nc.sbuf_tensor(name, shape, dt))

    def sem(name):
        return ctx.enter_context(nc.semaphore(name))

    raw = sb(ctx, "raw", [P, RAW_SLOTS, 2, 2 * NC])
    whi = sb(ctx, "whi", [P, AHEAD, 2 * NC], F32R)
    wlo = sb(ctx, "wlo", [P, AHEAD, 2 * NC], F32R)
    ident = sb(ctx, "ident", [P, P])
    gmix = sb(ctx, "gmix", [P, KD])
    cols = sb(ctx, "cols", [P, 8 * KF + NG])
    warm = sb(ctx, "warm", [P, TT])
    part = sb(ctx, "part", [P, 9, TT, 4])
    ssq = sb(ctx, "ssq", [P, 9, TT])
    var = sb(ctx, "var", [P, 9, TT])
    std = sb(ctx, "std", [P, 9, TT])
    rstd = sb(ctx, "rstd", [P, 9, TT])
    life_a = ExitStack()
    actA = sb(life_a, "actA", [P, 2, KD, S], F32R)
    mixmem = ExitStack()
    actB = sb(mixmem, "actB", [P, 2, KD, S], F32R)
    bufX = sb(mixmem, "bufX", [P, TT, D])
    bufY = sb(mixmem, "bufY", [P, TT, D])
    mix = ExitStack()
    lat = sb(mix, "lat", [P, 2, 2 * KL, S], F32R)
    mask = sb(mix, "mask", [P, 3 * P])
    cosT = sb(mix, "cosT", [P, TT, HALF])
    sinT = sb(mix, "sinT", [P, TT, HALF])
    kpeT = sb(mix, "kpeT", [ROPE, S])
    ropet = sb(mix, "ropet", [P, 4, TT * 2 * HALF])
    early = ExitStack()
    grow = sb(early, "grow", [NG, P])
    gmrow = sb(early, "gmrow", [KD, P])
    crow = sb(early, "crow", [2 * KF, 4, P])
    zlat = sb(early, "zlat", [P, 2, TT, QL])
    kpe = sb(early, "kpe", [P, TT, ROPE])
    pm0 = sb(early, "pm0", [P, 4, S])
    pm1 = sb(early, "pm1", [P, 4, P])
    pos_i = sb(early, "pos_i", [P, TT], I32)
    posf = sb(early, "posf", [P, TT])
    invf = sb(early, "invf", [P, HALF])
    ang = sb(early, "ang", [P, TT, HALF])
    turns = sb(early, "turns", [P, TT, HALF])
    early.close()
    pairs = ExitStack()
    q_sb = sb(pairs, "q_sb", [P, TT, QPAIR])
    kv_sb = sb(pairs, "kv_sb", [P, TT, NC])
    qkT = sb(pairs, "qkT", [P, 2, 2 * S])
    qpeT = sb(pairs, "qpeT", [ROPE, 2, S])
    prob = sb(pairs, "prob", [P, 2, 3 * P])
    probT = sb(pairs, "probT", [P, 2, 3 * P])
    gp_sb = sb(pairs, "gp_sb", [P, TT, NC])
    smax = sb(pairs, "smax", [P, 2, TT])
    nmax = sb(pairs, "nmax", [P, 2, TT])
    ssum = sb(pairs, "ssum", [P, 2, TT])
    rsum = sb(pairs, "rsum", [P, 2, TT])
    pairs.close()
    mix.close()
    memp = ExitStack()
    memk = sb(memp, "memk", [P, KD, S])
    memv = sb(memp, "memv", [P, TT, D])
    kch = sb(memp, "kch", [P, TT, NC])
    mmax = sb(memp, "mmax", [P, TT])
    mnmax = sb(memp, "mnmax", [P, TT])
    msum = sb(memp, "msum", [P, TT])
    mrsum = sb(memp, "mrsum", [P, TT])
    memp.close()
    mixmem.close()
    ffn = ExitStack()
    gT = sb(ffn, "gT", [P, 2, KF, S], F32R)
    a_sb = sb(ffn, "a_sb", [P, 2, TT, NC])
    cg = sb(ffn, "cg", [P, 4, S])
    cu = sb(ffn, "cu", [P, 4, S])
    ffn.close()
    life_a.close()
    tail = ExitStack()
    y3 = sb(tail, "y3", [P, TT, D])
    x3 = sb(tail, "x3", [P, TT, D])
    tail.close()
    ccol = cols[:, 0:8 * KF].rearrange("p (c f) -> p c f", c=4)
    gcol = cols[:, 8 * KF:8 * KF + NG]
    gpost = memv[:, 0, :]
    gpost3 = a_sb[:, :, :, :].rearrange("p a t n -> p (a t n)")
    mq_sb = bufY[:, :, 0:NC]
    mv_sb = bufY[:, :, NC:2 * NC]
    mp_sb = bufY[:, :, 2 * NC:2 * NC + S]
    mpT = bufY[:, :, 3 * NC:3 * NC + S]
    mqT = kch[:, :, :].rearrange("p t n -> p (t n)").rearrange("p (d s) -> p d s", s=S)

    bank = [ctx.enter_context(nc.psum_tensor(f"bank{i}", [P, 512], F32)) for i in range(8)]
    acc = bank[0:2]
    tr = bank[2:4]
    sc = bank[4:6]
    at = bank[6:8]
    four = bank[2:4] + bank[6:8]

    w_loaded = [sem(f"w_loaded{s}") for s in range(RAW_SLOTS)]
    hi_done, lo_done, w_used = sem("hi_done"), sem("lo_done"), sem("w_used")
    acc0_ready = sem("acc0_ready")
    acc_out = [sem("acc0_out"), sem("acc1_out")]
    t_filled, t_hi, t_out = sem("t_filled"), sem("t_hi"), sem("t_out")
    at_filled, at_out = sem("at_filled"), sem("at_out")
    x_in = [sem(f"x_in{q}") for q in range(ND)]
    gm_in, g_in, c_in, pos_in = sem("gm_in"), sem("g_in"), sem("c_in"), sem("pos_in")
    ident_ok, consts_ok, pm_ok, pm_step = sem("ident_ok"), sem("consts_ok"), sem("pm_ok"), sem("pm_step")
    part_zero = sem("part_zero")
    sq_done, sum_done, var_done, std_done, rstd_done = (sem(n) for n in (
        "sq_done", "sum_done", "var_done", "std_done", "rstd_done"))
    rope_step, trig_ok, abs_ok, rope_ok, ang_ok = (sem(n) for n in (
        "rope_step", "trig_ok", "abs_ok", "rope_ok", "ang_ok"))
    s_filled, s_max, s_nmax, s_exp, s_rsum, s_norm = (sem(n) for n in (
        "s_filled", "s_max", "s_nmax", "s_exp", "s_rsum", "s_norm"))
    mp_ok = sem("mp_ok")
    mrg_mul, mrg_ok = sem("mrg_mul"), sem("mrg_ok")
    mem_in, x_again, gpost_in = sem("mem_in"), sem("x_again"), sem("gpost_in")
    y_gained, res_done = sem("y_gained"), sem("res_done")
    mv_ok, m_filled, m_max, m_nmax, m_exp, m_rsum, m_norm = (sem(n) for n in (
        "mv_ok", "m_filled", "m_max", "m_nmax", "m_exp", "m_rsum", "m_norm"))
    y_scaled, pool_res = sem("y_scaled"), sem("pool_res")
    mpT_filled, mpT_out = sem("mpT_filled"), sem("mpT_out")
    spill, x3_in, stored = sem("spill"), sem("x3_in"), sem("stored")
    ga_filled, ua_filled, conv_step, gconv, uconv, gelu_ok, f_mul, f_hi, f_lo = (sem(n) for n in (
        "ga_filled", "ua_filled", "conv_step", "gconv", "uconv", "gelu_ok", "f_mul", "f_hi", "f_lo"))

    BY_POOL = (0, 1)

    def chunk_of(buf, q):
        return buf[:, q % 2, q // 2 * NC:(q // 2 + 1) * NC]

    def filled(f):
        return f + 1 if isinstance(f, int) and f < T_Y else f + 1 - 4

    def width(v):
        if V_KPE <= v < V_GRP:
            return 4 * ROPE
        if V_GRP <= v < V_YP:
            return 4 * P
        if v >= V_FOUT and (v - V_FOUT) % 6 == 1:
            return NC
        return 2 * NC

    def f32(ap):
        return ap.bitcast(F32)

    SQ = {}
    count = 0
    for n, parts in ((N_X, 8), (N_Q, 2), (N_C, 2), (N_MEM, 8), (N_Y1, 8), (N_X2, 8), (N_Y2, 8), (N_X3, 8), (N_Y3, 8)):
        SQ[n] = count
        count += parts

    block = ctx.enter_context(nc.Block())

    @block.sync
    def _(sp):
        def load(c, cs, src, n, kts=4):
            s = cs % RAW_SLOTS
            if not (isinstance(c, int) and c < RAW_SLOTS):
                sp.wait_ge(lo_done, 2 * c - 2 * RAW_SLOTS + 2)
            if n == NC:
                dst = raw[:, s, :, :].rearrange("p u (k n) -> p (u k) n", n=n)[:, 0:kts, :]
                sp.dma_start(dst, src).then_inc(w_loaded[s], 32)
            else:
                per = kts // 2
                for h in range(2):
                    dst = raw[:, s, h, 0:per * n].rearrange("p (k n) -> p k n", n=n)
                    sp.dma_start(dst, src[:, h * per:(h + 1) * per, :]).then_inc(w_loaded[s], 16)

        def x_quarter(q):
            sp.dma_start(bufX[:, :, q * NC:(q + 1) * NC], tok[:, :, q * NC:(q + 1) * NC]).then_inc(x_in[q], 16)

        def column(c, w, col, n=NC, kd=KD):
            for j in range(kd // 4):
                load(c + j, j, w[:, 4 * j:4 * j + 4, bass.ds(col, n)], n)

        for j, quarters in enumerate(((0,), (1, 2), (3,), ())):
            for q in quarters:
                x_quarter(q)
            load(j, j, w_in[:, 4 * j:4 * j + 4, C_Q:C_Q + NC], NC)
        for name, row, k in (("g_mem_pre", G_MEM, KD), ("g_mem_kv", G_MEMKV, KD), ("g_ffn_pre", G_FFN, KD),
                             ("g_q_a", G_Q, KL), ("g_kv_a", G_KV, KL), ("pool_scale", G_POOL, KP)):
            sp.dma_start(grow[row:row + k, :], a[name][0].rearrange("(k p) -> k p", p=P)).then_inc(g_in, 16)
        sp.dma_start(crow[:, 0:3, :], a["conv_w"][0].rearrange("c (f p) -> f c p", p=P)).then_inc(c_in, 16)
        sp.dma_start(crow[:, 3, :], a["conv_b"][0].rearrange("(f p) -> f p", p=P)).then_inc(c_in, 16)
        sp.dma_start(pos_i[:, :], a["positions"][0].rearrange("(t p) -> p t", p=P),
                     allow_slow_non_contiguous=True).then_inc(pos_in, 16)
        column(V_LAT // 2 + 4, w_in, C_Q + NC)
        for n in range(2):
            column(V_POOLIN // 2 + 4 * n, w_in, C_U + n * NC)
        for j in range(2):
            load(V_KPE // 2 + j, j, w_in[:, 8 * j:8 * j + 8, C_PE:C_PE + ROPE], ROPE, 8)
        for j in range(2):
            load(V_GRP // 2 + j, 2 + j, w_grp[:, 4 * j:4 * j + 4, :], 2 * P)
        with sp.Fori(0, ND // 2) as i:
            for m in range(2):
                for j in range(2):
                    load(V_YP // 2 + 4 * i + 2 * m + j, 2 * m + j,
                         rows("w_pool_br")[:, 4 * j:4 * j + 4, bass.ds(i * 2 * NC + m * NC, NC)], NC)
        with sp.Fori(0, NH // 4) as i:
            for m in range(2):
                c = V_ATT // 2 + 12 * i + 6 * m
                load(c, 6 * m, w_qb[:, :, bass.ds(i * 2 * QPAIR + m * QPAIR, QPAIR)], QPAIR)
                load(c + 1, 6 * m + 1, w_kvb[:, :, bass.ds(i * 2 * NC + m * NC, NC)], NC)
                for j in range(4):
                    load(c + 2 + j, 6 * m + 2 + j,
                         w_in[:, 4 * j:4 * j + 4, bass.ds(i * NC + (C_GA, C_GP)[m], NC)], NC)
        for name, v, n in (("w_attn_br", V_YA, ND), ("w_mix_out", V_MIX, ND), ("w_mem_kv", V_MKV, 2 * ND),
                           ("w_mem_q", V_MQ, ND), ("w_mem_o", V_MO, ND)):
            with sp.Fori(0, n) as i:
                column(v // 2 + 4 * i, rows(name), i * NC)
        with sp.Fori(0, NF) as i:
            for m in range(2):
                column(V_FIN // 2 + 8 * i + 4 * m, rows("w_ffn_in"), i * NC + m * DFF)
        with sp.Fori(0, ND) as i:
            k = 0
            for j in range(12):
                kts = (3, 4, 4)[j % 3]
                load(V_FOUT // 2 + 12 * i + j, j, rows("w_ffn_out")[:, k:k + kts, bass.ds(i * NC, NC)], NC, kts)
                k += kts
        by_dve = [q for q in range(8) if q not in BY_POOL]
        order = by_dve[:-2] + [BY_POOL[0]] + by_dve[-2:-1] + [BY_POOL[1]] + by_dve[-1:]
        for q in order:
            t, o = q % 2, slice(q // 2 * NC, (q // 2 + 1) * NC)
            if q in BY_POOL:
                sp.wait_ge(pool_res, BY_POOL.index(q) + 1)
            else:
                sp.wait_ge(res_done, 16 + by_dve.index(q) + 1)
            sp.dma_start(outtok[:, t, o], y3[:, t, o]).then_inc(stored, 16)
        sp.wait_ge(stored, 16 * 8)

    @block.gpsimd
    def _(pool):
        pool.memset(ident[:, :], 0.0).then_inc(pm_step, 1)
        pool.wait_ge(pm_step, 1)
        pool.affine_select(out=ident[:, :], in_=ident[:, :], compare_op=ALU.not_equal, fill=1.0, base=0,
                           pattern=[[-1, P]], channel_multiplier=1).then_inc(ident_ok, 1)
        freq = np.float32(THETA) ** (-np.arange(0, ROPE, 2, dtype=np.float32) / np.float32(ROPE))
        for j in range(HALF):
            last = pool.memset(invf[:, j:j + 1], float(freq[j]))
        last.then_inc(consts_ok, 1)
        for g, w in enumerate(WINDOWS):
            pool.memset(pm1[:, g, :], 1.0 / w)
            last = pool.memset(pm0[:, g, w - 1:S], 1.0 / w)
            for t in range(w - 1):
                last = pool.memset(pm0[:, g, t:t + 1], 1.0 / (t + 1))
        last.then_inc(pm_step, 1)
        pool.wait_ge(pm_step, 2)
        n = 2
        for g, w in enumerate(WINDOWS):
            for pm, queries in ((pm0, S), (pm1, P)):
                pool.affine_select(out=pm[:, g, :], in_=pm[:, g, :], compare_op=ALU.is_ge, fill=0.0, base=0,
                                   pattern=[[1, queries]], channel_multiplier=-1).then_inc(pm_step, 1)
                n += 1
                pool.wait_ge(pm_step, n)
                pool.affine_select(out=pm[:, g, :], in_=pm[:, g, :], compare_op=ALU.is_ge, fill=0.0, base=w - 1,
                                   pattern=[[-1, queries]], channel_multiplier=1).then_inc(pm_step, 1)
                n += 1
                pool.wait_ge(pm_step, n)
                pool.tensor_tensor(pm[:, g, 0:P], pm[:, g, 0:P], ident[:, :], ALU.subtract).then_inc(pm_ok, 1)
        pool.memset(mask[:, :], 0.0).then_inc(mp_ok, 1)
        pool.wait_ge(mp_ok, 1)
        for b in (0, 2):
            last = pool.affine_select(out=mask[:, b * P:(b + 1) * P], in_=mask[:, b * P:(b + 1) * P],
                                      compare_op=ALU.is_ge, fill=NEG, base=0, pattern=[[-1, P]],
                                      channel_multiplier=1)
            last.then_inc(consts_ok, 1)
        with pool.Fori(0, ND) as i:
            for t in range(TT):
                pool.wait_ge(acc_out[t], U_ATT + 6 * i + 6)
                ya = bufY[:, t, bass.ds(i * NC, NC)]
                pool.tensor_tensor(ya, ya, gp_sb[:, t, :], ALU.mult).then_inc(mp_ok, 1)

        def post(n, y, gain, k):
            pool.wait_ge(gpost_in, 16 * (k + 1))
            for j in range(ND):
                for t in range(TT):
                    pool.wait_ge(sq_done, SQ[n] + 2 * j + t + 1)
                    ya = y[:, t, j * NC:(j + 1) * NC]
                    pool.tensor_tensor(ya, ya, gain[:, j * NC:(j + 1) * NC], ALU.mult).then_inc(y_gained, 1)

        post(N_Y1, bufY, gpost, 0)
        with pool.Fori(0, ND) as i:
            pool.wait_ge(acc_out[0], U_MQ + 1 + i)
            pool.wait_ge(acc_out[1], U_MQ + 1 + i)
            pool.tensor_copy(mv_sb, memv[:, :, bass.ds(i * NC, NC)]).then_inc(mv_ok, 1)
        post(N_Y2, bufY, gpost, 1)
        post(N_Y3, y3, gpost3, 2)
        pool.wait_ge(x3_in, 16)
        for j, q in enumerate(BY_POOL):
            ya = chunk_of(y3, q)
            pool.wait_ge(y_scaled, j + 1)
            pool.tensor_tensor(ya, ya, chunk_of(x3, q), ALU.add).then_inc(pool_res, 1)

    @block.tensor
    def _(pe):
        def unit(v, vs, lhs, kts, n, u, first, last):
            s = vs % AHEAD
            pe.wait_ge(lo_done, v + 1)
            for t in range(TT):
                if first and not (isinstance(u, int) and u == 0):
                    pe.wait_ge(acc_out[t], u)
                for kk, k in enumerate(kts):
                    hi, lo = lhs(0, k)[:, t * P:(t + 1) * P], lhs(1, k)[:, t * P:(t + 1) * P]
                    wh, wl = whi[:, s, kk * n:(kk + 1) * n], wlo[:, s, kk * n:(kk + 1) * n]
                    f, l = first and kk == 0, last and kk == len(kts) - 1
                    pe.matmul(acc[t][:, 0:n], hi, wh, start=f, stop=False)
                    pe.matmul(acc[t][:, 0:n], hi, wl, start=False, stop=False)
                    mm = pe.matmul(acc[t][:, 0:n], lo, wh, start=False, stop=l)
                if last and t == 0:
                    mm.then_inc(acc0_ready, 1)
            mm.then_inc(w_used, 1)

        def lhsA(part_, k):
            return actA[:, part_, k, :]

        def lhsB(part_, k):
            return actB[:, part_, k, :]

        def t_wait(f):
            if not (isinstance(f, int) and f < 2):
                pe.wait_ge(t_out, f - 1)

        def t_fill(f, fs, src, k, banks=tr):
            if banks is tr:
                t_wait(f)
            elif fs >= 4:
                pe.wait_ge(t_out, f - 3)
            for j in range(2):
                for t in range(TT):
                    o = j * S + t * P
                    mm = pe.transpose(banks[fs % len(banks)][:, o:o + P],
                                      src[:, t, (k + j) * P:(k + j + 1) * P], ident[:, :])
            mm.then_inc(t_filled, 1)

        def at_wait(f):
            if not (isinstance(f, int) and f < 2):
                pe.wait_ge(at_out, f - 1)

        pe.wait_ge(ident_ok, 1)

        def keep_warm(times):
            for _ in range(times):
                pe.transpose(sc[0][:, 0:P], ident[:, :], ident[:, :])

        keep_warm(WARM_UP)
        pe.wait_ge(gm_in, 16)
        pe.transpose(sc[1][:, 0:KD], gmrow[:, :], ident[0:KD, 0:KD]).then_inc(at_filled, 1)

        def x_fill(k):
            if k % 2 == 0:
                pe.wait_ge(x_in[k // 2], 16)
            t_fill(T_X + k, k, bufX, 2 * k, four)

        for k in range(4):
            if k == 2:
                keep_warm(WARM_UP)
            x_fill(k)
        for v in range(16):
            if v < 8:
                pe.wait_ge(t_out, T_X + v + 1)
            unit(V_LAT + v, v, lhsA, (2 * (v % 8), 2 * (v % 8) + 1), NC, U_LAT + v // 8, v % 8 == 0, v % 8 == 7)
            if v < 4:
                x_fill(v + 4)
            if v == 8:
                pe.wait_ge(c_in, 32)
                pe.wait_ge(g_in, 16 * 6)
                for j in range(4):
                    pe.transpose(at[1][:, j * 2 * KF:(j + 1) * 2 * KF], crow[:, j, :], ident[0:2 * KF, 0:2 * KF])
                pe.transpose(at[1][:, 8 * KF:8 * KF + NG], grow[:, :], ident[0:NG, 0:NG]).then_inc(at_filled, 1)
            if v in (10, 12):
                pe.wait_ge(acc_out[0], U_LAT + 1)
                pe.wait_ge(acc_out[1], U_LAT + 1)
                t_fill(T_Q + (v - 10) // 2, (v - 10) // 2, zlat[:, 0, :, :], v - 10)
        for v in range(16):
            unit(V_POOLIN + v, v, lhsA, (2 * (v % 8), 2 * (v % 8) + 1), NC, U_POOLIN + v // 8, v % 8 == 0, v % 8 == 7)
            if v in (2, 4):
                pe.wait_ge(acc_out[0], U_LAT + 2)
                pe.wait_ge(acc_out[1], U_LAT + 2)
                t_fill(T_C + (v - 2) // 2, (v - 2) // 2, zlat[:, 1, :, :], v - 2)

        def pooled(f):
            t_wait(T_D + f)
            for j in range(2):
                k = 2 * f + j
                o = j * S
                pe.matmul(tr[f % 2][:, o:o + S], bufY[:, 0, k * P:(k + 1) * P], pm0[:, f, :], start=True, stop=False)
                mm = pe.matmul(tr[f % 2][:, o + P:o + S], bufY[:, 1, k * P:(k + 1) * P], pm1[:, f, :],
                               start=False, stop=True)
            mm.then_inc(t_filled, 1)

        pe.wait_ge(pm_ok, 8)
        for v in range(4):
            unit(V_KPE + v, v, lhsA, range(4 * v, 4 * v + 4), ROPE, U_KPE, v == 0, v == 3)
            if v == 0:
                for t in range(TT):
                    pe.wait_ge(acc_out[t], U_POOLIN + 2)
                pooled(0)
                pooled(1)
            if v == 2:
                pooled(2)
                pooled(3)
        for g in range(4):
            pe.wait_ge(lo_done, V_GRP + g + 1)
            pe.wait_ge(t_out, T_D + g + 1)
            if g < 2:
                t_wait(T_Y + g)
            s = (V_GRP + g) % AHEAD
            for j in range(2):
                dst = four[g][:, j * S:(j + 1) * S]
                for c in range(2):
                    o = c * 2 * P + j * P
                    wh, wl = whi[:, s, o:o + P], wlo[:, s, o:o + P]
                    dh, dl = lhsB(0, 2 * g + c), lhsB(1, 2 * g + c)
                    pe.matmul(dst, wh, dh, start=(c == 0), stop=False)
                    pe.matmul(dst, wl, dh, start=False, stop=False)
                    mm = pe.matmul(dst, wh, dl, start=False, stop=(c == 1))
            mm.then_inc(w_used, 1)
        with pe.Fori(0, ND // 2) as i:
            for m in range(2):
                for k in range(4):
                    if m == 0:
                        pe.wait_ge(t_out, T_Y + k + 1)
                    unit(V_YP + 8 * i + 4 * m + k, 4 * m + k,
                         lambda h, kt: lhsB(h, KP + kt), (2 * k, 2 * k + 1), NC, U_YP + 2 * i + m, k == 0, k == 3)
        pe.wait_ge(rope_ok, 1)
        for t in range(TT):
            mm = pe.transpose(at[A_KPE % 2][0:ROPE, t * P:(t + 1) * P], kpe[:, t, :], ident[:, :])
        mm.then_inc(at_filled, 1)
        with pe.Fori(0, NH // 4) as i:
            for m in range(2):
                v, u, f = V_ATT + 24 * i + 12 * m, U_ATT + 6 * i + 3 * m, A_PAIR + 10 * i + 5 * m
                pair, fs = 2 * i + m, A_PAIR + 5 * m
                for k in range(12):
                    if k < 2:
                        unit(v + k, k, lambda h, kt: lat[:, h, kt, :], (2 * k, 2 * k + 1), QPAIR, u, k == 0, k == 1)
                    elif k < 4:
                        unit(v + k, k, lambda h, kt: lat[:, h, KL + kt, :], (2 * k - 4, 2 * k - 3), NC, u + 1,
                             k == 2, k == 3)
                    else:
                        unit(v + k, k, lhsA, (2 * k - 8, 2 * k - 7), NC, u + 2, k == 4, k == 11)
                    if k in (5, 6):
                        h = k - 5
                        for t in range(TT):
                            pe.wait_ge(acc_out[t], u + 2)
                        at_wait(f + h)
                        if k == 6:
                            pe.wait_ge(rope_ok, pair + 2)
                            at_wait(f + 2)
                        for t in range(TT):
                            pe.transpose(at[(fs + h) % 2][:, t * P:(t + 1) * P],
                                         q_sb[:, t, h * (NOPE + ROPE):h * (NOPE + ROPE) + NOPE], ident[:, :])
                            mm = pe.transpose(at[(fs + h) % 2][:, S + t * P:S + (t + 1) * P],
                                              kv_sb[:, t, 2 * h * P:(2 * h + 1) * P], ident[:, :])
                        mm.then_inc(at_filled, 1)
                    if k == 6:
                        for h in range(2):
                            o = h * (NOPE + ROPE) + NOPE
                            for t in range(TT):
                                mm = pe.transpose(at[fs % 2][0:ROPE, h * S + t * P:h * S + (t + 1) * P],
                                                  q_sb[:, t, o:o + ROPE], ident[:, :])
                        mm.then_inc(at_filled, 1)
                    if k in (7, 8):
                        h = k - 7
                        pe.wait_ge(at_out, f + 3)
                        for t in range(TT):
                            w = (t + 1) * P
                            dst = sc[h][:, t * P:t * P + w]
                            pe.matmul(dst, qkT[:, h, t * P:(t + 1) * P], qkT[:, h, S:S + w], start=True, stop=False)
                            mm = pe.matmul(dst, qpeT[:, h, t * P:(t + 1) * P], kpeT[:, 0:w], start=False, stop=True)
                        mm.then_inc(s_filled, 1)
                    if k in (9, 10):
                        h = k - 9
                        pe.wait_ge(s_norm, 4 * pair + 2 * h + 2)
                        at_wait(f + 3 + h)
                        for b in range(3):
                            mm = pe.transpose(at[(fs + 3 + h) % 2][:, b * P:(b + 1) * P],
                                              prob[:, h, b * P:(b + 1) * P], ident[:, :])
                        mm.then_inc(at_filled, 1)
                    if k == 11:
                        pe.wait_ge(at_out, f + 5)
                        t_wait(T_O + pair)
                        for h in range(2):
                            vcol = slice((2 * h + 1) * P, (2 * h + 2) * P)
                            dst = tr[(T_O + m) % 2]
                            pe.matmul(dst[:, h * S:(h + 1) * S], kv_sb[:, 0, vcol], probT[:, h, 0:S],
                                      start=True, stop=False)
                            mm = pe.matmul(dst[:, h * S + P:(h + 1) * S], kv_sb[:, 1, vcol], probT[:, h, S:S + P],
                                           start=False, stop=True)
                        mm.then_inc(t_filled, 1)

        def column(v, u, lhs, job):
            for k in range(8):
                unit(v + k, k, lhs, (2 * k, 2 * k + 1), NC, u, k == 0, k == 7)
                job(k)

        def nothing(k):
            pass

        def merged(n):
            def job(k):
                if k in (2, 3):
                    pe.wait_ge(mrg_ok, 2 * n + 2)
                    t_fill(T_MRG + 2 * n + k - 2, k - 2, kch, 2 * (k - 2))
            return job

        def lhs_o(h, k):
            return actB[:, h, k, :]

        def ya_column(n, job):
            for k in range(8):
                if isinstance(n, int) and n == 0 and k == 6:
                    pe.wait_ge(t_out, T_O + 8)
                unit(V_YA + 8 * n + k, k, lhs_o, (2 * k, 2 * k + 1), NC, U_YA + n, k == 0, k == 7)
                job(k)

        pe.wait_ge(t_out, T_O + 7)
        ya_column(0, nothing)
        with pe.Fori(1, ND) as n:
            ya_column(n, merged(n - 1))

        for k in range(8):
            if k < 6 and k % 2 == 0:
                pe.wait_ge(t_out, T_MRG + k + 2)
            if k == 6:
                pe.wait_ge(t_out, T_MRG + 8)
            unit(V_MIX + k, k, lhsA, (2 * k, 2 * k + 1), NC, U_MIX, k == 0, k == 7)
            merged(ND - 1)(k)

        def mem_job(k):
            if k == 0:
                pe.wait_ge(mem_in, 16)
            t_fill(T_MEM + k, k, memv, 2 * k)

        column(V_MIX + 8, U_MIX + 1, lhsA, mem_job)
        with pe.Fori(2, ND) as n:
            column(V_MIX + 8 * n, U_MIX + n, lhsA, nothing)

        def mk_job(n):
            def job(k):
                if k == 1:
                    for t in range(TT):
                        pe.wait_ge(acc_out[t], U_MKV + n + 1)
                    for b in range(2):
                        at_wait(A_MK + 2 * n + b)
                        for j in range(2):
                            for t in range(TT):
                                mm = pe.transpose(at[(A_MK + b) % 2][:, j * S + t * P:j * S + (t + 1) * P],
                                                  kch[:, t, (2 * b + j) * P:(2 * b + j + 1) * P], ident[:, :])
                        mm.then_inc(at_filled, 1)
            return job

        pe.wait_ge(t_out, T_MEM + 8)
        column(V_MKV, U_MKV, lhsB, nothing)
        with pe.Fori(1, ND) as n:
            column(V_MKV + 8 * n, U_MKV + n, lhsB, mk_job(n - 1))

        def x2_job(k):
            pe.wait_ge(res_done, 8)
            t_fill(T_X2 + k, k, bufX, 2 * k)
            mk_job(ND - 1)(k)

        column(V_MKV + 8 * ND, U_MKV + ND, lhsB, x2_job)
        with pe.Fori(ND + 1, 2 * ND) as n:
            column(V_MKV + 8 * n, U_MKV + n, lhsB, nothing)

        def mem_head(n):
            def job(k):
                if k == 0:
                    for t in range(TT):
                        pe.wait_ge(acc_out[t], U_MQ + n + 1)
                    for b in range(2):
                        at_wait(A_MQ + 2 * n + b)
                        for j in range(2):
                            for t in range(TT):
                                mm = pe.transpose(at[(A_MQ + b) % 2][:, j * S + t * P:j * S + (t + 1) * P],
                                                  mq_sb[:, t, (2 * b + j) * P:(2 * b + j + 1) * P], ident[:, :])
                        mm.then_inc(at_filled, 1)
                if k == 1:
                    pe.wait_ge(at_out, A_MQ + 2 * n + 2)
                    for t in range(TT):
                        for d in range(4):
                            mm = pe.matmul(sc[0][:, t * S:(t + 1) * S], mqT[:, d, t * P:(t + 1) * P],
                                           memk[:, 4 * n + d, :], start=(d == 0), stop=(d == 3))
                    mm.then_inc(m_filled, 1)
                if k == 4:
                    pe.wait_ge(m_norm, 2 * n + 2)
                    for b in range(2):
                        for t in range(TT):
                            mm = pe.transpose(sc[1][:, b * S + t * P:b * S + (t + 1) * P],
                                              mp_sb[:, t, b * P:(b + 1) * P], ident[:, :])
                    mm.then_inc(mpT_filled, 1)
                if k in (5, 6):
                    pe.wait_ge(mpT_out, n + 1)
                    pe.wait_ge(mv_ok, n + 1)
                    t_wait(T_MOUT + 2 * n + k - 5)
                    for j in range(2):
                        d = 2 * (k - 5) + j
                        for b in range(2):
                            mm = pe.matmul(tr[(k - 5) % 2][:, j * S:(j + 1) * S], mv_sb[:, b, d * P:(d + 1) * P],
                                           mpT[:, b, :], start=(b == 0), stop=(b == 1))
                    mm.then_inc(t_filled, 1)
            return job

        pe.wait_ge(t_out, T_X2 + 8)
        column(V_MQ, U_MQ, lhsA, nothing)
        with pe.Fori(1, ND) as n:
            column(V_MQ + 8 * n, U_MQ + n, lhsA, mem_head(n - 1))
        pe.wait_ge(t_out, T_MOUT + 6)
        for k in range(8):
            if k == 6:
                mem_head(ND - 1)(6)
            if k >= 6:
                pe.wait_ge(t_out, T_MOUT + k + 1)
            unit(V_MO + k, k, lhs_o, (2 * k, 2 * k + 1), NC, U_MO, k == 0, k == 7)
            if k != 6:
                mem_head(ND - 1)(k)
        with pe.Fori(1, ND) as n:
            column(V_MO + 8 * n, U_MO + n, lhs_o, nothing)

        def a_fill(m, i, banks, done):
            for t in range(TT):
                pe.wait_ge(acc_out[t], U_FIN + 2 * i + m + 1)
            if m == 1 or not isinstance(i, int) or i > 0:
                pe.wait_ge(gconv, 2 * i + 2 * m)
            for b in range(2):
                for j in range(2):
                    for t in range(TT):
                        mm = pe.transpose(banks[b][:, j * S + t * P:j * S + (t + 1) * P],
                                          a_sb[:, m, t, (2 * b + j) * P:(2 * b + j + 1) * P], ident[:, :])
                mm.then_inc(done, 1)

        def ffn_turn(i, first):
            for k in range(16):
                if first and k < 8:
                    pe.wait_ge(t_out, T_X3 + k + 1)
                unit(V_FIN + 16 * i + k, k, lhsA, (2 * (k % 8), 2 * (k % 8) + 1), NC, U_FIN + 2 * i + k // 8,
                     k % 8 == 0, k % 8 == 7)
                if first and k < 4:
                    x3_fill(k + 4)
                if k == 1 and not first:
                    a_fill(1, i - 1, at, ua_filled)
                if k == 9:
                    a_fill(0, i, sc, ga_filled)

        def x3_fill(k):
            if k % 2 == 0:
                pe.wait_ge(res_done, 8 + k + 2)
            t_fill(T_X3 + k, k, bufX, 2 * k, four)

        for k in range(4):
            x3_fill(k)
        ffn_turn(0, True)
        with pe.Fori(1, NF) as i:
            ffn_turn(i, False)

        def lhsG(h, k):
            return gT[:, h, k, :]

        def fout(n, first):
            k0 = 0
            for k in range(24):
                kc = (2, 1, 2, 2, 2, 2)[k % 6]
                if first and k0 <= 4 * (NF - 1) < k0 + kc:
                    pe.wait_ge(f_lo, 2 * NF)
                unit(V_FOUT + 24 * n + k, k, lhsG, range(k0, k0 + kc), NC, U_FOUT + n, k == 0, k == 23)
                k0 += kc
                if first and k == 1:
                    a_fill(1, NF - 1, at, ua_filled)

        pe.wait_ge(f_lo, 2 * NF - 2)
        fout(0, True)
        with pe.Fori(1, ND) as n:
            fout(n, False)

    @block.scalar
    def _(act):
        def hi(v, vs):
            if isinstance(v, int) and v >= N_UNITS:
                return
            c = (vs // 2) % RAW_SLOTS
            turn = v // 8 if isinstance(v, int) else None
            act.wait_ge(w_loaded[c], 32 * (turn + 1))
            if v >= AHEAD:
                act.wait_ge(w_used, v - AHEAD + 1)
            w = width(v)
            act.activation(whi[:, vs % AHEAD, 0:w], raw[:, c, vs % 2, 0:w], ACT.Copy).then_inc(hi_done, 1)

        def hi_at(base, i, per, k):
            ks = base + k + AHEAD
            c = (ks // 2) % RAW_SLOTS
            if isinstance(i, int):
                v = ks + per * i
                if v < N_UNITS:
                    hi(v, v)
                return
            act.wait_ge(w_loaded[c], 32 * (ks // 8 + 1) + i * (4 * per))
            act.wait_ge(w_used, base + k + 1 + i * per)
            w = width(ks)
            act.activation(whi[:, ks % AHEAD, 0:w], raw[:, c, ks % 2, 0:w], ACT.Copy).then_inc(hi_done, 1)

        def evac(u, v, dst, n=None, width=NC, func=ACT.Copy):
            if n is not None:
                act.wait_ge(rstd_done, n + 1)
            for t in range(TT):
                if t == 0:
                    act.wait_ge(acc0_ready, u + 1)
                else:
                    act.wait_ge(w_used, v + 1)
                scale = 1.0 if n is None else rstd[:, n, t:t + 1]
                act.activation(dst[t], acc[t][:, 0:width], func, scale=scale).then_inc(acc_out[t], 1)

        def square(n, k, src, dst=None):
            j, t = k // 2, k % 2
            if SQ[n] + k > 0:
                act.wait_ge(sq_done, SQ[n] + k)
            act.activation(sc[0][:, :], src, ACT.Square,
                           accum_out=part[:, n, t, j:j + 1] if dst is None else dst).then_inc(sq_done, 1)

        def root(n):
            act.wait_ge(var_done, n + 1)
            act.activation(std[:, n, :], var[:, n, :], ACT.Sqrt).then_inc(std_done, 1)

        def t_split(f, fs, dst, scale=None, ready=None, banks=tr, gains=gcol):
            if ready is None:
                act.wait_ge(t_filled, filled(f))
            else:
                act.wait_ge(w_used, ready)
            for j in range(2):
                act.activation(dst[j], banks[fs % len(banks)][:, j * S:(j + 1) * S], ACT.Copy,
                               scale=1.0 if scale is None else gains[:, scale + j:scale + j + 1]).then_inc(t_hi, 1)

        def at_copy(f, fs, dst, width=512, parts=P):
            act.wait_ge(at_filled, f + 1)
            act.activation(dst, at[fs % 2][0:parts, 0:width], ACT.Copy).then_inc(at_out, 1)

        act.dma_start(gmrow[:, :], a["g_mix_pre"][0].rearrange("(k p) -> k p", p=P)).then_inc(gm_in, 16)
        act.wait_ge(at_filled, 1)
        act.activation(gmix[:, :], sc[1][:, 0:KD], ACT.Copy).then_inc(at_out, 1)
        act.wait_ge(at_out, 1)

        def x_split(k):
            t_split(T_X + k, k, [actA[:, 0, 2 * k + j, :] for j in range(2)], 2 * k, banks=four, gains=gmix)

        for k in (0, 2):
            x_split(k)
            x_split(k + 1)
            hi(k, k)
            hi(k + 1, k + 1)
        act.wait_ge(part_zero, 1)
        for k in range(16):
            if k < 4:
                x_split(k + 4)
            if k % 8 == 7:
                evac(U_LAT + k // 8, V_LAT + k, [zlat[:, k // 8, t, :] for t in range(TT)], N_X)
            if k == 5:
                root(N_X)
            hi_at(V_LAT, 0, 16, k)
            if k < 4:
                act.wait_ge(x_in[k], 16)
                for t in range(TT):
                    square(N_X, 2 * k + t, bufX[:, t, k * NC:(k + 1) * NC])
            if k == 15:
                act.wait_ge(ang_ok, 1)
                act.activation(sinT[:, :, :], ang[:, :, :], ACT.Sin).then_inc(trig_ok, 1)
                act.activation(cosT[:, :, :], turns[:, :, :], ACT.Sin).then_inc(trig_ok, 1)
            if k % 8 == 7:
                for t in range(TT):
                    act.wait_ge(acc_out[t], U_LAT + k // 8 + 1)
                    square(N_Q + k // 8, t, zlat[:, k // 8, t, :])
            if k == 8:
                at_copy(A_SET + 1, 1, cols[:, :], 8 * KF + NG)
                root(N_Q)
            if k in (10, 12):
                act.wait_ge(at_out, 2)
                f = (k - 10) // 2
                t_split(T_Q + f, f, [lat[:, 0, 2 * f + j, :] for j in range(2)], G_Q + 2 * f)
        for k in range(16):
            if k % 8 == 7:
                evac(U_POOLIN + k // 8, V_POOLIN + k,
                     [bufY[:, t, k // 8 * NC:(k // 8 + 1) * NC] for t in range(TT)], N_X)
            hi_at(V_POOLIN, 0, 16, k)
            if k == 0:
                root(N_C)
            if k in (2, 4):
                f = (k - 2) // 2
                t_split(T_C + f, f, [lat[:, 0, KL + 2 * f + j, :] for j in range(2)], G_KV + 2 * f)
        for k in range(8):
            if k == 3:
                evac(U_KPE, V_KPE + 3, [kpe[:, t, :] for t in range(TT)], N_X, ROPE)
            if k >= 4:
                g = k - 4
                t_split(T_Y + g, g, [actB[:, 0, KP + 2 * g + j, :] for j in range(2)], G_POOL + 2 * g,
                        V_GRP + g + 1, banks=four)
            hi_at(V_KPE, 0, 8, k)
            if k in (0, 2):
                for f in (k, k + 1):
                    t_split(T_D + f, f, [actB[:, 0, 2 * f + j, :] for j in range(2)])
        with act.Fori(0, ND // 2) as i:
            for m in range(2):
                for k in range(4):
                    if k == 3:
                        evac(U_YP + 2 * i + m, V_YP + 8 * i + 4 * m + 3,
                             [bufY[:, t, bass.ds(i * 2 * NC + m * NC, NC)] for t in range(TT)])
                    hi_at(V_YP, i, 8, 4 * m + k)
        at_copy(A_KPE, A_KPE, kpeT[:, :], S, ROPE)
        with act.Fori(0, NH // 4) as i:
            for m in range(2):
                v, u, f = V_ATT + 24 * i + 12 * m, U_ATT + 6 * i + 3 * m, A_PAIR + 10 * i + 5 * m
                pair, fs = 2 * i + m, A_PAIR + 5 * m
                for k in range(12):
                    if k == 1:
                        evac(u, v + 1, [q_sb[:, t, :] for t in range(TT)], N_Q, QPAIR)
                    if k == 3:
                        evac(u + 1, v + 3, [kv_sb[:, t, :] for t in range(TT)], N_C)
                    if k == 11 and m == 0:
                        evac(u + 2, v + 11, [bufX[:, t, bass.ds(i * NC, NC)] for t in range(TT)], N_X,
                             func=ACT.Sigmoid)
                    if k == 11 and m == 1:
                        act.wait_ge(mp_ok, 2 * i + 1)
                        evac(u + 2, v + 11, [gp_sb[:, t, :] for t in range(TT)], N_X, func=ACT.Sigmoid)
                    hi_at(V_ATT, i, 24, 12 * m + k)
                    if k == 5:
                        at_copy(f, fs, qkT[:, 0, :])
                    if k == 6:
                        at_copy(f + 1, fs + 1, qkT[:, 1, :])
                        at_copy(f + 2, fs, qpeT[:, :, :].rearrange("p h s -> p (h s)"), 512, ROPE)
                    if k in (8, 9):
                        h = k - 8
                        act.wait_ge(s_nmax, 2 * pair + h + 1)
                        for t in range(TT):
                            pr = prob[:, h, t * P:(2 * t + 1) * P]
                            act.activation(pr, pr, ACT.Exp, bias=nmax[:, h, t:t + 1], scale=SCALE,
                                           accum_out=ssum[:, h, t:t + 1]).then_inc(s_exp, 1)
                    if k in (9, 10):
                        at_copy(f + k - 6, fs + k - 6, probT[:, k - 9, :], 3 * P)
                    if k == 11:
                        t_split(T_O + pair, T_O + m, [actB[:, 0, 4 * i + 2 * m + j, :] for j in range(2)])

        def merged(n):
            def job(k):
                if k in (2, 3):
                    t_split(T_MRG + 2 * n + k - 2, k - 2, [actA[:, 0, 4 * n + 2 * (k - 2) + j, :] for j in range(2)])
            return job

        def nothing(k):
            pass

        def branch_out(u, n, v, dst, y):
            for t in range(TT):
                if t == 0:
                    act.wait_ge(acc0_ready, u + n + 1)
                else:
                    act.wait_ge(w_used, v + 1)
                act.activation(dst[t], acc[t][:, :], ACT.Copy).then_inc(acc_out[t], 1)
                act.wait_ge(acc_out[t], u + n + 1)
                act.wait_ge(sq_done, SQ[y] + 2 * n + t)
                act.activation(sc[0][:, :], dst[t], ACT.Square,
                               accum_out=part[:, y, t, bass.ds(n, 1)]).then_inc(sq_done, 1)

        def prewarm(n):
            act.activation(warm[:, :], var[:, n, :], ACT.Sqrt)

        def column(base, u, n, dst, norm, job, y=None):
            for k in range(8):
                if k == 7 and y is None:
                    evac(u + n, base + 8 * n + 7, dst, norm)
                if k == 7 and y is not None:
                    branch_out(u, n, base + 8 * n + 7, dst, y)
                    if y == N_Y2 and isinstance(n, int) and n == ND - 1:
                        root(y)
                hi_at(base, n, 8, k)
                job(k)

        def chunk(buf, n):
            return [buf[:, t, bass.ds(n * NC, NC)] for t in range(TT)]

        kch_t = [kch[:, t, :] for t in range(TT)]
        act.wait_ge(mp_ok, 2 * ND + 1)
        column(V_YA, U_YA, 0, kch_t, None, nothing)
        act.wait_ge(t_out, T_O + 8)
        act.dma_start(memv[:, :, :], memtok).then_inc(mem_in, 16)
        with act.Fori(1, ND) as n:
            column(V_YA, U_YA, n, kch_t, None, merged(n - 1))

        def mem_squares(k):
            if k == 0:
                act.wait_ge(mem_in, 16)
            for q in (k,) if k < 6 else (6, 7) if k == 6 else ():
                square(N_MEM, q, memv[:, q % 2, q // 2 * NC:(q // 2 + 1) * NC])
            merged(ND - 1)(k)
            if k == 2:
                act.wait_ge(mrg_ok, 2 * ND)
                act.dma_start(bufX[:, :, :], tok).then_inc(x_again, 16)

        column(V_MIX, U_MIX, 0, chunk(bufY, 0), None, mem_squares, y=N_Y1)

        def mem_split(k):
            if k == 0:
                root(N_MEM)
            t_split(T_MEM + k, k, [actB[:, 0, 2 * k + j, :] for j in range(2)], G_MEMKV + 2 * k)
            if k == 7:
                act.dma_start(gpost, a["g_mix_post"].broadcast_to([P, D])).then_inc(gpost_in, 16)

        column(V_MIX, U_MIX, 1, chunk(bufY, 1), None, mem_split, y=N_Y1)
        with act.Fori(2, ND) as n:
            column(V_MIX, U_MIX, n, chunk(bufY, n), None, nothing, y=N_Y1)

        def x2_squares(k):
            if k == 0:
                root(N_Y1)
            for q in ([] if k == 0 else [k - 1] if k < 7 else [6, 7]):
                act.wait_ge(res_done, q + 1)
                square(N_X2, q, bufX[:, q % 2, q // 2 * NC:(q // 2 + 1) * NC])

        def mk_job(n):
            def job(k):
                if k == 1:
                    for b in range(2):
                        at_copy(A_MK + 2 * n + b, A_MK + b,
                                memk[:, bass.ds(4 * n + 2 * b, 2), :].rearrange("p k s -> p (k s)"))
            return job

        column(V_MKV, U_MKV, 0, kch_t, N_MEM, x2_squares)
        with act.Fori(1, ND) as n:
            column(V_MKV, U_MKV, n, kch_t, N_MEM, mk_job(n - 1))

        def x2_split(k):
            if k == 0:
                root(N_X2)
            t_split(T_X2 + k, k, [actA[:, 0, 2 * k + j, :] for j in range(2)], G_MEM + 2 * k)
            mk_job(ND - 1)(k)

        column(V_MKV, U_MKV, ND, chunk(memv, 0), N_MEM, x2_split)
        with act.Fori(ND + 1, 2 * ND) as n:
            column(V_MKV, U_MKV, n, chunk(memv, n - ND), N_MEM, nothing)

        def mem_head(n):
            def job(k):
                if k == 0:
                    for b in range(2):
                        at_copy(A_MQ + 2 * n + b, A_MQ + b, mqT[:, 2 * b:2 * b + 2, :].rearrange("p k s -> p (k s)"))
                if k == 2:
                    act.wait_ge(m_nmax, n + 1)
                    for t in range(TT):
                        act.activation(mp_sb[:, t, :], sc[0][:, t * S:(t + 1) * S], ACT.Exp, bias=mnmax[:, t:t + 1],
                                       scale=MSCALE, accum_out=msum[:, t:t + 1]).then_inc(m_exp, 1)
                if k == 4:
                    act.wait_ge(mpT_filled, n + 1)
                    act.activation(mpT, sc[1][:, :].rearrange("p (b s) -> p b s", b=2), ACT.Copy).then_inc(mpT_out, 1)
                if k in (5, 6):
                    t_split(T_MOUT + 2 * n + k - 5, k - 5,
                            [actB[:, 0, 4 * n + 2 * (k - 5) + j, :] for j in range(2)])
            return job

        mq_t = [mq_sb[:, t, :] for t in range(TT)]
        column(V_MQ, U_MQ, 0, mq_t, N_X2, nothing)
        with act.Fori(1, ND) as n:
            column(V_MQ, U_MQ, n, mq_t, N_X2, mem_head(n - 1))

        def last_head(k):
            if k == 5:
                mem_head(ND - 1)(5)
                mem_head(ND - 1)(6)
                act.wait_ge(mv_ok, ND)
                act.dma_start(gpost, a["g_mem_post"].broadcast_to([P, D])).then_inc(gpost_in, 16)
            elif k != 6:
                mem_head(ND - 1)(k)

        column(V_MO, U_MO, 0, chunk(bufY, 0), None, last_head, y=N_Y2)
        with act.Fori(1, ND - 1) as n:
            column(V_MO, U_MO, n, chunk(bufY, n), None, nothing, y=N_Y2)
        column(V_MO, U_MO, ND - 1, chunk(bufY, ND - 1), None, lambda k: prewarm(N_X2) if k == 6 else None, y=N_Y2)

        def up_hi(i, b):
            act.wait_ge(f_mul, 2 * i + b + 1)
            act.activation(gT[:, 0, bass.ds(4 * i + 2 * b, 2), :], cu[:, 2 * b:2 * b + 2, :],
                           ACT.Copy).then_inc(f_hi, 1)

        def ffn_turn(i, first):
            for k in range(16):
                if first and k < 4:
                    x3_split(k + 4)
                if first and k < 8:
                    for q in ((0, 1), (2, 3), (4,), (5,), (6,), (7,), (), ())[k]:
                        act.wait_ge(res_done, 8 + q + 1)
                        square(N_X3, q, bufX[:, q % 2, q // 2 * NC:(q // 2 + 1) * NC])
                if k % 8 == 7:
                    m = k // 8
                    evac(U_FIN + 2 * i + m, V_FIN + 16 * i + k, [a_sb[:, m, t, :] for t in range(TT)], N_X3)
                if first and k == 6:
                    root(N_X3)
                hi_at(V_FIN, i, 16, k)
                if first and k == 6:
                    act.wait_ge(res_done, 16)
                    act.dma_start(x3_spill.rearrange("(t p) d -> p t d", p=P), bufX[:, :, :]).then_inc(spill, 16)
                if not first and k in (3, 5):
                    up_hi(i - 1, k // 4)
                if k == 13:
                    act.wait_ge(gconv, 2 * i + 2)
                    g = cg[:, :, :].rearrange("p f s -> p (f s)")
                    act.activation(g, g, ACT.Gelu_apprx_tanh).then_inc(gelu_ok, 1)

        def x3_split(k):
            t_split(T_X3 + k, k, [actA[:, 0, 2 * k + j, :] for j in range(2)], G_FFN + 2 * k, banks=four)

        for k in range(4):
            x3_split(k)
        ffn_turn(0, True)
        act.wait_ge(spill, 16)
        with act.Fori(1, NF) as i:
            ffn_turn(i, False)

        def fout(n, first):
            for k in range(24):
                if k == 23:
                    branch_out(U_FOUT, n, V_FOUT + 24 * n + 23, chunk(y3, n), N_Y3)
                if not (isinstance(n, int) and n == ND - 1 and k >= 20):
                    hi_at(V_FOUT, n, 24, k)
                if first and k == 0:
                    act.wait_ge(w_used, V_FOUT)
                    act.dma_start(x3[:, :, :], x3_spill.rearrange("(t p) d -> p t d", p=P)).then_inc(x3_in, 16)
                if first and k in (3, 5):
                    up_hi(NF - 1, k // 4)
                if first and k == 6:
                    act.wait_ge(ua_filled, 2 * NF)
                    act.dma_start(gpost3, a["g_ffn_post"].broadcast_to([P, D])).then_inc(gpost_in, 16)
                if isinstance(n, int) and n == ND - 1 and k == 22:
                    prewarm(N_X3)

        fout(0, True)
        with act.Fori(1, ND - 1) as n:
            fout(n, False)
        fout(ND - 1, False)
        root(N_Y3)
        act.wait_ge(rstd_done, N_Y3 + 1)
        for q in BY_POOL:
            t = q % 2
            act.wait_ge(y_gained, 16 + q + 1)
            act.activation(chunk_of(y3, q), chunk_of(y3, q), ACT.Copy,
                           scale=rstd[:, N_Y3, t:t + 1]).then_inc(y_scaled, 1)

    @block.vector
    def _(dve):
        def lo(v, vs):
            c, w = (vs // 2) % RAW_SLOTS, width(vs)
            dve.wait_ge(hi_done, v + 1)
            dve.tensor_tensor(wlo[:, vs % AHEAD, 0:w], raw[:, c, vs % 2, 0:w], f32(whi[:, vs % AHEAD, 0:w]),
                              ALU.subtract).then_inc(lo_done, 1)

        def lo_at(base, i, per, k):
            v = base + k + AHEAD + i * per
            if isinstance(v, int) and v >= N_UNITS:
                return
            lo(v, base + k + AHEAD if not isinstance(v, int) else v)

        def t_split(f, fs, hi_, lo_, scale=None, banks=tr, gains=gcol):
            dve.wait_ge(t_hi, 2 * f + 2)
            for j in range(2):
                src = banks[fs % len(banks)][:, j * S:(j + 1) * S]
                if scale is None:
                    op = dve.tensor_tensor(lo_[j], src, f32(hi_[j]), ALU.subtract)
                else:
                    op = dve.scalar_tensor_tensor(out=lo_[j], in0=src, scalar=gains[:, scale + j:scale + j + 1],
                                                  in1=f32(hi_[j]), op0=ALU.mult, op1=ALU.subtract)
            op.then_inc(t_out, 1)

        def tiles(buf, k):
            return [[buf[:, h, k + j, :] for j in range(2)] for h in range(2)]

        def norm(n, parts, width=D):
            dve.wait_ge(sq_done, SQ[n] + parts)
            dve.tensor_reduce(ssq[:, n, :], part[:, n, :, :], AX.X, ALU.add).then_inc(sum_done, 1)
            dve.wait_ge(sum_done, n + 1)
            dve.tensor_scalar(var[:, n, :], ssq[:, n, :], 1.0 / width, EPS, ALU.mult, ALU.add).then_inc(var_done, 1)
            dve.wait_ge(std_done, n + 1)
            dve.reciprocal(rstd[:, n, :], std[:, n, :]).then_inc(rstd_done, 1)

        steps = [0]

        def step(op):
            op.then_inc(rope_step, 1)
            steps[0] += 1
            dve.wait_ge(rope_step, steps[0])

        def rotate(xs, first_step, rotations):
            if not isinstance(rotations, int):
                dve.wait_ge(rope_ok, rotations)
            for h, x in enumerate(xs):
                x1, x2 = x[:, :, 0:HALF], x[:, :, HALF:ROPE]
                dve.tensor_tensor(rope_part(h, 0), x1, cosT[:, :, :], ALU.mult)
                dve.tensor_tensor(rope_part(h, 1), x2, sinT[:, :, :], ALU.mult)
                dve.tensor_tensor(rope_part(h, 2), x2, cosT[:, :, :], ALU.mult)
                last = dve.tensor_tensor(rope_part(h, 3), x1, sinT[:, :, :], ALU.mult)
            last.then_inc(rope_step, 1)
            dve.wait_ge(rope_step, first_step + 1)
            for h, x in enumerate(xs):
                dve.tensor_tensor(x[:, :, 0:HALF], rope_part(h, 0), rope_part(h, 1), ALU.subtract)
                last = dve.tensor_tensor(x[:, :, HALF:ROPE], rope_part(h, 2), rope_part(h, 3), ALU.add)
            last.then_inc(rope_ok, 1)

        def rope_part(h, j):
            return ropet[:, j, h * TT * HALF:(h + 1) * TT * HALF].rearrange("p (t c) -> p t c", t=TT)

        dve.memset(part[:, :, :, :], 0.0).then_inc(part_zero, 1)
        dve.wait_ge(at_out, 1)

        def x_split(k):
            t_split(T_X + k, k, *tiles(actA, 2 * k), 2 * k, four, gmix)

        for k in (0, 2):
            x_split(k)
            x_split(k + 1)
            lo(k, k)
            lo(k + 1, k + 1)
        for k in range(16):
            if k < 4:
                x_split(k + 4)
            if k == 5:
                norm(N_X, 8)
            lo_at(V_LAT, 0, 16, k)
            if k == 14:
                dve.wait_ge(pos_in, 16)
                dve.wait_ge(consts_ok, 1)
                step(dve.tensor_copy(posf[:, :], pos_i[:, :]))
                for t in range(TT):
                    step(dve.tensor_scalar(ang[:, t, :], invf[:, :], posf[:, t:t + 1], None, ALU.mult))
                step(dve.tensor_scalar(turns[:, :, :], ang[:, :, :], float(1 / (2 * np.pi)), ROUND, ALU.mult, ALU.add))
                step(dve.tensor_scalar(turns[:, :, :], turns[:, :, :], ROUND, None, ALU.subtract))
                for c in (TWO_PI_A, TWO_PI_B, TWO_PI_C):
                    step(dve.scalar_tensor_tensor(out=ang[:, :, :], in0=turns[:, :, :], scalar=-c,
                                                  in1=ang[:, :, :], op0=ALU.mult, op1=ALU.add))
                step(dve.tensor_scalar(ang[:, :, :], ang[:, :, :], 3.1415925, -3.1415925, ALU.min, ALU.max))
                step(dve.scalar_tensor_tensor(out=turns[:, :, :], in0=ang[:, :, :], scalar=-1.0, in1=ang[:, :, :],
                                              op0=ALU.mult, op1=ALU.min))
                dve.tensor_scalar(turns[:, :, :], turns[:, :, :], float(np.pi / 2), None, ALU.add).then_inc(ang_ok, 1)
            if k == 8:
                norm(N_Q, 2, QL)
            if k in (10, 12):
                dve.wait_ge(at_out, 2)
                t_split(T_Q + (k - 10) // 2, (k - 10) // 2, *tiles(lat, k - 10), G_Q + k - 10)
        for k in range(16):
            lo_at(V_POOLIN, 0, 16, k)
            if k == 0:
                norm(N_C, 2, QL)
            if k in (2, 4):
                t_split(T_C + (k - 2) // 2, (k - 2) // 2, *tiles(lat, KL + k - 2), G_KV + k - 2)
        for k in range(8):
            if k >= 4:
                t_split(T_Y + k - 4, k - 4, *tiles(actB, KP + 2 * (k - 4)), G_POOL + 2 * (k - 4), four)
            lo_at(V_KPE, 0, 8, k)
            if k in (0, 2):
                for f in (k, k + 1):
                    t_split(T_D + f, f, *tiles(actB, 2 * f))
        dve.wait_ge(trig_ok, 2)
        for t in range(TT):
            dve.wait_ge(acc_out[t], U_KPE + 1)
        rotate([kpe[:, :, :]], steps[0], 0)
        steps[0] += 1
        with dve.Fori(0, ND // 2) as i:
            for k in range(8):
                lo_at(V_YP, i, 8, k)
        dve.wait_ge(consts_ok, 3)
        with dve.Fori(0, NH // 4) as i:
            for m in range(2):
                u, pair = U_ATT + 6 * i + 3 * m, 2 * i + m

                def row_max(h):
                    n = 2 * pair + h
                    dve.wait_ge(s_filled, n + 1)
                    dve.tensor_tensor(prob[:, h, 0:P], sc[h][:, 0:P], mask[:, 0:P], ALU.add).then_inc(s_max, 1)
                    dve.tensor_tensor_reduce(prob[:, h, P:3 * P], sc[h][:, P:3 * P], mask[:, P:3 * P], 1.0, -3.0e38,
                                             ALU.add, ALU.max, smax[:, h, 1:2]).then_inc(s_max, 1)
                    dve.wait_ge(s_max, 3 * n + 1)
                    dve.tensor_reduce(smax[:, h, 0:1], prob[:, h, 0:P], AX.X, ALU.max).then_inc(s_max, 1)
                    dve.wait_ge(s_max, 3 * n + 3)
                    dve.tensor_scalar(nmax[:, h, :], smax[:, h, :], -SCALE, None, ALU.mult).then_inc(s_nmax, 1)

                def normalise(h):
                    n = 2 * pair + h
                    dve.wait_ge(s_exp, 2 * n + 2)
                    dve.reciprocal(rsum[:, h, :], ssum[:, h, :]).then_inc(s_rsum, 1)
                    dve.wait_ge(s_rsum, n + 1)
                    for t in range(TT):
                        o = slice(t * P, (2 * t + 1) * P)
                        dve.tensor_scalar(prob[:, h, o], prob[:, h, o], rsum[:, h, t:t + 1], None,
                                          ALU.mult).then_inc(s_norm, 1)

                for k in range(12):
                    lo_at(V_ATT, i, 24, 12 * m + k)
                    if k == 3:
                        for t in range(TT):
                            dve.wait_ge(acc_out[t], u + 1)
                        rotate([q_sb[:, :, o:o + ROPE] for o in (NOPE, 2 * NOPE + ROPE)], steps[0] + pair, pair + 1)
                    if k == 7:
                        row_max(0)
                    if k == 8:
                        row_max(1)
                        normalise(0)
                    if k == 9:
                        normalise(1)
                    if k == 11:
                        t_split(T_O + pair, T_O + m, *tiles(actB, 4 * i + 2 * m))

        def column(base, n, job, ahead=()):
            for k in range(8):
                if k in ahead:
                    job(k)
                lo_at(base, n, 8, k)
                if k not in ahead:
                    job(k)

        def nothing(k):
            pass

        def merge(n):
            def job(k):
                if k == 0:
                    for t in range(TT):
                        dve.wait_ge(acc_out[t], U_YA + n + 1)
                        dve.wait_ge(mp_ok, 2 * ND + 1)
                        y, g, b = (kch[:, t, :], bufX[:, t, bass.ds(n * NC, NC)], bufY[:, t, bass.ds(n * NC, NC)])
                        dve.tensor_tensor(y, y, g, ALU.mult).then_inc(mrg_mul, 1)
                        dve.wait_ge(mrg_mul, 2 * n + t + 1)
                        dve.tensor_tensor(y, y, b, ALU.add).then_inc(mrg_ok, 1)
                if k in (2, 3):
                    t_split(T_MRG + 2 * n + k - 2, k - 2, *tiles(actA, 4 * n + 2 * (k - 2)))
            return job

        column(V_YA, 0, nothing)
        with dve.Fori(1, ND) as n:
            column(V_YA, n, merge(n - 1))
        column(V_MIX, 0, merge(ND - 1))

        def mem_split(k):
            if k == 0:
                norm(N_MEM, 8)
            t_split(T_MEM + k, k, *tiles(actB, 2 * k), G_MEMKV + 2 * k)

        column(V_MIX, 1, mem_split)
        with dve.Fori(2, ND) as n:
            column(V_MIX, n, nothing)

        def residual(n, q, y, x, dst, gained):
            t, o = q % 2, slice(q // 2 * NC, (q // 2 + 1) * NC)
            dve.wait_ge(y_gained, gained + q + 1)
            dve.scalar_tensor_tensor(out=dst[:, t, o], in0=y[:, t, o], scalar=rstd[:, n, t:t + 1], in1=x[:, t, o],
                                     op0=ALU.mult, op1=ALU.add).then_inc(res_done, 1)

        def x2_job(k):
            if k == 0:
                norm(N_Y1, 8)
                dve.wait_ge(rstd_done, N_Y1 + 1)
                dve.wait_ge(x_again, 16)
            residual(N_Y1, k, bufY, bufX, bufX, 0)

        column(V_MKV, 0, x2_job)
        with dve.Fori(1, ND) as n:
            column(V_MKV, n, nothing)

        def x2_split(k):
            if k == 0:
                norm(N_X2, 8)
            t_split(T_X2 + k, k, *tiles(actA, 2 * k), G_MEM + 2 * k)

        column(V_MKV, ND, x2_split)
        with dve.Fori(ND + 1, 2 * ND) as n:
            column(V_MKV, n, nothing)

        def mem_head(n):
            def job(k):
                if k == 1:
                    dve.wait_ge(m_filled, n + 1)
                    dve.tensor_reduce(mmax[:, :], sc[0][:, :].rearrange("p (t s) -> p t s", t=TT), AX.X,
                                      ALU.max).then_inc(m_max, 1)
                    dve.wait_ge(m_max, n + 1)
                    dve.tensor_scalar(mnmax[:, :], mmax[:, :], -MSCALE, None, ALU.mult).then_inc(m_nmax, 1)
                if k == 3:
                    dve.wait_ge(m_exp, 2 * n + 2)
                    dve.reciprocal(mrsum[:, :], msum[:, :]).then_inc(m_rsum, 1)
                    dve.wait_ge(m_rsum, n + 1)
                    for t in range(TT):
                        dve.tensor_scalar(mp_sb[:, t, :], mp_sb[:, t, :], mrsum[:, t:t + 1], None,
                                          ALU.mult).then_inc(m_norm, 1)
                if k in (5, 6):
                    t_split(T_MOUT + 2 * n + k - 5, k - 5, *tiles(actB, 4 * n + 2 * (k - 5)))
            return job

        column(V_MQ, 0, nothing)
        with dve.Fori(1, ND) as n:
            column(V_MQ, n, mem_head(n - 1), (3,))

        def last_head(k):
            if k == 5:
                mem_head(ND - 1)(5)
                mem_head(ND - 1)(6)
            elif k != 6:
                mem_head(ND - 1)(k)

        column(V_MO, 0, last_head, (3,))
        with dve.Fori(1, ND - 1) as n:
            column(V_MO, n, nothing)
        for k in range(8):
            if k == 7:
                norm(N_Y2, 8)
                dve.wait_ge(rstd_done, N_Y2 + 1)
                for q in range(4):
                    residual(N_Y2, q, bufY, bufX, bufX, 8)
            lo_at(V_MO, ND - 1, 8, k)

        def conv(src, dst, col, first_step, done):
            tile = [(src[:, j * S:(j + 1) * S], dst[:, j, :],
                     [ccol[:, c, bass.ds(col + j, 1)] for c in range(4)]) for j in range(2)]
            for x, y, w in tile:
                dve.tensor_scalar(y, x, w[2], w[3], ALU.mult, ALU.add).then_inc(conv_step, 1)
            for j, (x, y, w) in enumerate(tile):
                dve.wait_ge(conv_step, first_step + j + 1)
                dve.scalar_tensor_tensor(out=y[:, 1:S], in0=x[:, 0:S - 1], scalar=w[1], in1=y[:, 1:S],
                                         op0=ALU.mult, op1=ALU.add).then_inc(conv_step, 1)
            for j, (x, y, w) in enumerate(tile):
                dve.wait_ge(conv_step, first_step + j + 3)
                last = dve.scalar_tensor_tensor(out=y[:, 2:S], in0=x[:, 0:S - 2], scalar=w[0], in1=y[:, 2:S],
                                                op0=ALU.mult, op1=ALU.add)
            last.then_inc(done, 1)

        def up_conv(i, b):
            u = cu[:, 2 * b:2 * b + 2, :]
            dve.wait_ge(ua_filled, 2 * i + b + 1)
            dve.wait_ge(gelu_ok, i + 1)
            conv(at[b], u, 4 * i + KF + 2 * b, 16 * i + 8 + 4 * b, uconv)
            dve.wait_ge(uconv, 2 * i + b + 1)
            dve.tensor_tensor(u, u, cg[:, 2 * b:2 * b + 2, :], ALU.mult).then_inc(f_mul, 1)

        def up_lo(i, b):
            dve.wait_ge(f_hi, 2 * i + b + 1)
            g = [gT[:, h, bass.ds(4 * i + 2 * b, 2), :] for h in range(2)]
            dve.tensor_tensor(g[1], cu[:, 2 * b:2 * b + 2, :], f32(g[0]), ALU.subtract).then_inc(f_lo, 1)

        def up_job(i, k):
            if k in (1, 3):
                up_conv(i, k // 2)
            if k in (4, 6):
                up_lo(i, k // 2 - 2)

        def ffn_turn(i, first):
            for k in range(16):
                if first and k == 0:
                    for q in (6, 7):
                        residual(N_Y2, q, bufY, bufX, bufX, 8)
                if first and k < 4:
                    x3_split(k + 4)
                if first and k == 6:
                    norm(N_X3, 8)
                lo_at(V_FIN, i, 16, k)
                if not first:
                    up_job(i - 1, k)
                if k in (9, 11):
                    b = k // 2 - 4
                    dve.wait_ge(ga_filled, 2 * i + b + 1)
                    conv(sc[b], cg[:, 2 * b:2 * b + 2, :], 4 * i + 2 * b, 16 * i + 4 * b, gconv)

        def x3_split(k):
            t_split(T_X3 + k, k, *tiles(actA, 2 * k), G_FFN + 2 * k, four)

        x3_split(0)
        x3_split(1)
        for q in (4, 5):
            residual(N_Y2, q, bufY, bufX, bufX, 8)
        x3_split(2)
        x3_split(3)
        ffn_turn(0, True)
        with dve.Fori(1, NF) as i:
            ffn_turn(i, False)

        def fout(n, first):
            for k in range(24):
                if not (isinstance(n, int) and n == ND - 1 and k >= 20):
                    lo_at(V_FOUT, n, 24, k)
                if first:
                    up_job(NF - 1, k)

        fout(0, True)
        with dve.Fori(1, ND - 1) as n:
            fout(n, False)
        fout(ND - 1, False)
        norm(N_Y3, 8)
        dve.wait_ge(rstd_done, N_Y3 + 1)
        dve.wait_ge(x3_in, 16)
        for q in range(8):
            if q not in BY_POOL:
                residual(N_Y3, q, y3, x3, y3, 16)

    ctx.close()


_INS = ["x", "mem", "positions", "g_mix_pre", "w_in", "g_q_a", "w_q_b", "g_kv_a", "w_kv_b", "w_attn_br",
        "w_pool_grp", "pool_scale", "w_pool_br", "w_mix_out", "g_mix_post", "g_mem_pre", "g_mem_kv", "w_mem_q",
        "w_mem_kv", "w_mem_o", "g_mem_post", "g_ffn_pre", "w_ffn_in", "conv_w", "conv_b", "w_ffn_out", "g_ffn_post"]


def kernel(**inputs):
    import concourse.bacc as _bacc
    from concourse.bass_utils import run_bass_kernel_spmd as _run

    nc = _bacc.Bacc("TRN2", target_bir_lowering=False, num_devices=1)
    arrays, aps = {}, {}
    for name in _INS:
        v = np.ascontiguousarray(inputs[name])
        arrays[f"in_{name}"] = v
        aps[name] = nc.dram_tensor(f"in_{name}", v.shape, mybir.dt.from_np(v.dtype), kind="ExternalInput").ap()
    shape = inputs["x"].shape
    out = nc.dram_tensor("out_x", shape, F32, kind="ExternalOutput").ap()
    spill = nc.dram_tensor("x3_spill", shape[1:], F32, kind="Internal").ap()
    hybrid_layer(nc, aps, out, spill)
    r = _run(nc, [arrays], core_ids=[0])
    return r.results[0]["out_x"]
```
